# Optimizing a Trainium2 kernel written in Bass

```python
import math
import jax
import jax.numpy as jnp
from jax import lax
import numpy as np

D_MODEL = 1024
BATCH = 1
SEQ = 512
DEPTH = 2

CTX_LEN = 256
GRID_W = 64
N_MIXERS = 2
N_A_LAYERS = (DEPTH + N_MIXERS - 1) // N_MIXERS
N_B_LAYERS = DEPTH // N_MIXERS

DN_HEADS = 8
DN_HEAD_DIM = D_MODEL // DN_HEADS
DN_INNER = DN_HEADS * DN_HEAD_DIM
DN_CONV = 5
DN_CHUNK = 64
DN_PROJ = 4 * DN_INNER + 4 * DN_HEADS

DA_HEADS = 8
DA_HEAD_DIM = D_MODEL // (2 * DA_HEADS)
DA_INNER = 2 * DA_HEADS * DA_HEAD_DIM
DA_QBLOCK = 128
ROPE_BASE = 10000.0

PEER_HEADS = 8
PEER_NKEYS = 128
PEER_NEXPERTS = PEER_NKEYS * PEER_NKEYS
PEER_DKEY = 256
PEER_TOPK = 16
PEER_TOKBLOCK = 128
PEER_V_SCALE = 0.5

ADA_SCALE = 0.5
EPS = 1e-6

kernel_name = 'hybrid_deltanet_diffattn_peer_dit'

def rms_norm(x, g):
    xf = x.astype(jnp.float32)
    y = xf * lax.rsqrt(jnp.mean(xf * xf, axis=-1, keepdims=True) + EPS)
    return (y * g.astype(jnp.float32)).astype(x.dtype)

def l2_norm(x):
    xf = x.astype(jnp.float32)
    return xf * lax.rsqrt(jnp.sum(xf * xf, axis=-1, keepdims=True) + EPS)

def modulate(h, shift, scale):
    return h * (1 + scale) + shift

def ada_modulation(cond, w_mod, b_mod):
    m = jax.nn.silu(cond) @ w_mod + b_mod
    return jnp.split(m[..., None, :], 6, axis=-1)

def depthwise_conv_centred(x, w):
    k = w.shape[0]
    return lax.conv_general_dilated(
        x, w[:, None, :].astype(x.dtype), window_strides=(1,),
        padding=[(k // 2, k // 2)], dimension_numbers=('NWC', 'WIO', 'NWC'),
        feature_group_count=x.shape[-1])

def gated_delta_chunked(q, k, v, beta, g, s0):
    f32 = jnp.float32
    b_, h_, L, dk = q.shape
    dv = v.shape[-1]
    c_ = DN_CHUNK
    n = L // c_
    q, k, v = (t.astype(f32).reshape(b_, h_, n, c_, -1) for t in (q, k, v))
    beta = beta.astype(f32).reshape(b_, h_, n, c_)
    G = jnp.cumsum(g.astype(f32).reshape(b_, h_, n, c_), axis=-1)
    idx = jnp.arange(c_)
    lower = idx[:, None] >= idx[None, :]
    gam = jnp.exp(jnp.where(lower, G[..., :, None] - G[..., None, :], -jnp.inf))
    kb = k * beta[..., None]
    a_mat = jnp.where(idx[:, None] > idx[None, :],
                      jnp.einsum('bhnid,bhnjd->bhnij', kb, k) * gam, 0.0)
    rhs = jnp.concatenate([v * beta[..., None], kb * jnp.exp(G)[..., None]], axis=-1)
    sol = lax.linalg.triangular_solve(a_mat + jnp.eye(c_, dtype=f32), rhs,
                                      left_side=True, lower=True, unit_diagonal=True)
    u, w = sol[..., :dv], sol[..., dv:]
    qk = jnp.einsum('bhnid,bhnjd->bhnij', q, k) * gam
    q_dec = q * jnp.exp(G)[..., None]
    k_dec = k * jnp.exp(G[..., -1:] - G)[..., None]
    last_decay = jnp.exp(G[..., -1])

    def step(s, inp):
        u_c, w_c, qk_c, qd_c, kd_c, ld_c = inp
        delta = u_c - w_c @ s
        o_c = qd_c @ s + qk_c @ delta
        s = s * ld_c[..., None, None] + jnp.einsum('bhcd,bhce->bhde', kd_c, delta)
        return s, o_c

    xs = tuple(jnp.moveaxis(t, 2, 0) for t in (u, w, qk, q_dec, k_dec, last_decay))
    s_final, o = lax.scan(step, s0.astype(f32), xs)
    return jnp.moveaxis(o, 0, 2).reshape(b_, h_, L, dv), s_final

def time_flip(t, direction):
    return t if direction == 0 else jnp.flip(t, axis=2)

def deltanet_mixer(a_ctx, a_lat, w_in, conv_w, a_log, dt_bias, norm_g, w_out, ctx_out):
    def project(h):
        b_, L, _ = h.shape
        p = h @ w_in
        qkv = jax.nn.silu(depthwise_conv_centred(p[..., :3 * DN_INNER], conv_w))
        qkv = jnp.moveaxis(qkv.reshape(b_, L, 3, DN_HEADS, DN_HEAD_DIM), 1, 3)
        q = l2_norm(qkv[:, 0]) * DN_HEAD_DIM ** -0.5
        k = l2_norm(qkv[:, 1])
        v = qkv[:, 2]
        z = p[..., 3 * DN_INNER:4 * DN_INNER].reshape(b_, L, DN_HEADS, DN_HEAD_DIM)
        ab = p[..., 4 * DN_INNER:].astype(jnp.float32).reshape(b_, L, 2, 2, DN_HEADS)
        beta = jax.nn.sigmoid(ab[:, :, 0])
        g = -jnp.exp(a_log.astype(jnp.float32)) * jax.nn.softplus(
            ab[:, :, 1] + dt_bias.astype(jnp.float32))
        return q, k, v, z, jnp.transpose(beta, (2, 0, 3, 1)), jnp.transpose(g, (2, 0, 3, 1))

    qc, kc, vc, zc, bc, gc = project(a_ctx)
    ql, kl, vl, zl, bl, gl = project(a_lat)
    outs_ctx, outs_lat = [], []
    for d in range(2):
        s0 = jnp.zeros(qc.shape[:2] + (DN_HEAD_DIM, DN_HEAD_DIM), jnp.float32)
        o_c, s_c = gated_delta_chunked(time_flip(qc, d), time_flip(kc, d), time_flip(vc, d),
                                       time_flip(bc[d], d), time_flip(gc[d], d), s0)
        o_l, _ = gated_delta_chunked(time_flip(ql, d), time_flip(kl, d), time_flip(vl, d),
                                     time_flip(bl[d], d), time_flip(gl[d], d), s_c)
        outs_ctx.append(time_flip(o_c, d))
        outs_lat.append(time_flip(o_l, d))

    def output(o, z):
        b_, L = z.shape[:2]
        o = jnp.swapaxes(o, 1, 2).astype(z.dtype)
        o = rms_norm(o, norm_g) * jax.nn.silu(z)
        return o.reshape(b_, L, DN_INNER) @ w_out

    m_lat = output(outs_lat[0] + outs_lat[1], zl)
    m_ctx = output(outs_ctx[0] + outs_ctx[1], zc) if ctx_out else None
    return m_ctx, m_lat

def axial_rope(rows, head_dim):
    f32 = jnp.float32
    quarter = head_dim // 4
    inv_freq = ROPE_BASE ** (-jnp.arange(quarter, dtype=f32) / quarter)
    r = jnp.broadcast_to(jnp.arange(rows, dtype=f32)[:, None], (rows, GRID_W)).reshape(-1)
    col = jnp.broadcast_to(jnp.arange(GRID_W, dtype=f32)[None, :], (rows, GRID_W)).reshape(-1)
    ang = jnp.concatenate([r[:, None] * inv_freq, col[:, None] * inv_freq], axis=-1)
    return jnp.cos(ang), jnp.sin(ang)

def apply_rope(x, cos, sin):
    x1, x2 = jnp.split(x.astype(jnp.float32), 2, axis=-1)
    c, s = cos[:, None, None, :], sin[:, None, None, :]
    return jnp.concatenate([x1 * c - x2 * s, x1 * s + x2 * c], axis=-1).astype(x.dtype)

def diff_softmax_attend(q, k, v, lam):
    s = jnp.einsum('bqhcd,bkhcd->bhcqk', q, k).astype(jnp.float32)
    p = jax.nn.softmax(s, axis=-1)
    w = p[:, :, 0] - lam * p[:, :, 1]
    return jnp.einsum('bhqk,bkhe->bqhe', w.astype(v.dtype), v)

def diff_attn_mixer(a_ctx, a_lat, w_qkv, q_norm_g, k_norm_g, lam_vecs, subln_g, w_out,
                    lambda_init, cos, sin, ctx_out):
    d = DA_HEAD_DIM
    b_, L, _ = a_lat.shape
    n_ctx = a_ctx.shape[1]

    def heads_qk(t, n, gain):
        return rms_norm(t.reshape(b_, n, DA_HEADS, 2, d), gain)

    p_lat = a_lat @ w_qkv
    q_l = apply_rope(heads_qk(p_lat[..., :DA_INNER], L, q_norm_g) * d ** -0.5, cos, sin)
    k_l = apply_rope(heads_qk(p_lat[..., DA_INNER:2 * DA_INNER], L, k_norm_g), cos, sin)
    v_l = p_lat[..., 2 * DA_INNER:].reshape(b_, L, DA_HEADS, 2 * d)
    p_ctx = a_ctx @ (w_qkv if ctx_out else w_qkv[:, DA_INNER:])
    k_c = heads_qk(p_ctx[..., -2 * DA_INNER:-DA_INNER], n_ctx, k_norm_g)
    v_c = p_ctx[..., -DA_INNER:].reshape(b_, n_ctx, DA_HEADS, 2 * d)
    lv = lam_vecs.astype(jnp.float32)
    lam = jnp.exp(jnp.sum(lv[0] * lv[1])) - jnp.exp(jnp.sum(lv[2] * lv[3])) + lambda_init

    k_all = jnp.concatenate([k_c, k_l], axis=1)
    v_all = jnp.concatenate([v_c, v_l], axis=1)
    nb = L // DA_QBLOCK
    q_blocks = jnp.moveaxis(q_l.reshape(b_, nb, DA_QBLOCK, DA_HEADS, 2, d), 1, 0)
    o_l = lax.map(lambda qb: diff_softmax_attend(qb, k_all, v_all, lam), q_blocks)
    o_l = jnp.moveaxis(o_l, 0, 1).reshape(b_, L, DA_HEADS, 2 * d)

    def output(o, n):
        o = rms_norm(o, subln_g) * (1.0 - lambda_init)
        return o.reshape(b_, n, DA_INNER) @ w_out

    m_lat = output(o_l, L)
    m_ctx = None
    if ctx_out:
        q_c = heads_qk(p_ctx[..., :DA_INNER], n_ctx, q_norm_g) * d ** -0.5
        m_ctx = output(diff_softmax_attend(q_c, k_c, v_c, lam), n_ctx)
    return m_ctx, m_lat

def peer_ffn(h, w_q, sub_keys, u_tab, v_tab):
    t_, dm = h.shape
    half = PEER_DKEY // 2

    def block(hb):
        tb = hb.shape[0]
        q = (hb @ w_q).reshape(tb, PEER_HEADS, 2, half)
        s = jnp.einsum('thpd,hpnd->thpn', q, sub_keys).astype(jnp.float32)
        s_top, i_top = lax.top_k(s, PEER_TOPK)
        cand_s = (s_top[:, :, 0, :, None] + s_top[:, :, 1, None, :]).reshape(tb, PEER_HEADS, -1)
        cand_i = (i_top[:, :, 0, :, None] * PEER_NKEYS + i_top[:, :, 1, None, :]).reshape(tb, PEER_HEADS, -1)
        best_s, best_pos = lax.top_k(cand_s, PEER_TOPK)
        expert = jnp.take_along_axis(cand_i, best_pos, axis=-1)
        gate = jax.nn.softmax(best_s, axis=-1)
        u_e = jnp.take(u_tab, expert, axis=0)
        v_e = jnp.take(v_tab, expert, axis=0)
        act = jax.nn.gelu(jnp.einsum('thkd,td->thk', u_e, hb), approximate=False)
        return jnp.einsum('thk,thkd->td', (gate * act).astype(hb.dtype), v_e)

    out = lax.map(block, h.reshape(t_ // PEER_TOKBLOCK, PEER_TOKBLOCK, dm))
    return out.reshape(t_, dm)

def setup_inputs(seed: int = 0) -> dict:
    key = jax.random.key(seed)
    ks = jax.random.split(key, 24)
    f32 = jnp.float32

    def nrm(k, shape, scale):
        return jax.random.normal(k, shape, f32) * scale

    def gain(k, shape):
        return 1.0 + 0.02 * jax.random.normal(k, shape, f32)

    dt = jnp.exp(jax.random.uniform(ks[11], (N_A_LAYERS, 2, DN_HEADS), f32,
                                    minval=math.log(1e-3), maxval=math.log(1e-1)))
    return {
        'x': nrm(ks[0], (BATCH, SEQ, D_MODEL), 1.0),
        'c': nrm(ks[1], (BATCH, D_MODEL), 1.0),
        'ctx': nrm(ks[2], (BATCH, CTX_LEN, D_MODEL), 1.0),
        'c_ctx': nrm(ks[3], (D_MODEL,), 1.0),
        'ada_w': nrm(ks[4], (DEPTH, D_MODEL, 6 * D_MODEL), ADA_SCALE * D_MODEL ** -0.5),
        'ada_b': nrm(ks[5], (DEPTH, 6 * D_MODEL), 0.02),
        'norm1_g': gain(ks[6], (DEPTH, D_MODEL)),
        'norm2_g': gain(ks[7], (DEPTH, D_MODEL)),
        'dn_w_in': nrm(ks[8], (N_A_LAYERS, D_MODEL, DN_PROJ), D_MODEL ** -0.5),
        'dn_conv': nrm(ks[9], (N_A_LAYERS, DN_CONV, 3 * DN_INNER), DN_CONV ** -0.5),
        'dn_a_log': jnp.log(jax.random.uniform(ks[10], (N_A_LAYERS, 2, DN_HEADS), f32,
                                               minval=1.0, maxval=16.0)),
        'dn_dt_bias': dt + jnp.log(-jnp.expm1(-dt)),
        'dn_norm_g': gain(ks[12], (N_A_LAYERS, DN_HEAD_DIM)),
        'dn_w_out': nrm(ks[13], (N_A_LAYERS, DN_INNER, D_MODEL), DN_INNER ** -0.5),
        'da_w_qkv': nrm(ks[14], (N_B_LAYERS, D_MODEL, 3 * DA_INNER), D_MODEL ** -0.5),
        'da_q_norm_g': gain(ks[15], (N_B_LAYERS, DA_HEAD_DIM)),
        'da_k_norm_g': gain(ks[16], (N_B_LAYERS, DA_HEAD_DIM)),
        'da_lambda': nrm(ks[17], (N_B_LAYERS, 4, DA_HEAD_DIM), 0.1),
        'da_subln_g': gain(ks[18], (N_B_LAYERS, 2 * DA_HEAD_DIM)),
        'da_w_out': nrm(ks[19], (N_B_LAYERS, DA_INNER, D_MODEL), DA_INNER ** -0.5),
        'peer_wq': nrm(ks[20], (DEPTH, D_MODEL, PEER_HEADS * PEER_DKEY), D_MODEL ** -0.5),
        'peer_keys': nrm(ks[21], (DEPTH, PEER_HEADS, 2, PEER_NKEYS, PEER_DKEY // 2),
                         (PEER_DKEY // 2) ** -0.5),
        'peer_u': nrm(ks[22], (DEPTH, PEER_NEXPERTS, D_MODEL), D_MODEL ** -0.5),
        'peer_v': nrm(ks[23], (DEPTH, PEER_NEXPERTS, D_MODEL), PEER_V_SCALE),
    }

def reference(x, c, ctx, c_ctx, ada_w, ada_b, norm1_g, norm2_g,
              dn_w_in, dn_conv, dn_a_log, dn_dt_bias, dn_norm_g, dn_w_out,
              da_w_qkv, da_q_norm_g, da_k_norm_g, da_lambda, da_subln_g, da_w_out,
              peer_wq, peer_keys, peer_u, peer_v):
    b_, L, dm = x.shape
    n_ctx = ctx.shape[1]
    rows = L // GRID_W
    cos, sin = axial_rope(rows, DA_HEAD_DIM)
    h_lat, h_ctx = x, ctx
    for i in range(DEPTH):
        last = i == DEPTH - 1
        sh1, sc1, gt1, sh2, sc2, gt2 = ada_modulation(c, ada_w[i], ada_b[i])
        csh1, csc1, cgt1, csh2, csc2, cgt2 = ada_modulation(c_ctx, ada_w[i], ada_b[i])
        a_lat = modulate(rms_norm(h_lat, norm1_g[i]), sh1, sc1)
        a_ctx = modulate(rms_norm(h_ctx, norm1_g[i]), csh1, csc1)
        j = i // N_MIXERS
        if i % N_MIXERS == 0:
            m_ctx, m_lat = deltanet_mixer(a_ctx, a_lat, dn_w_in[j], dn_conv[j], dn_a_log[j],
                                          dn_dt_bias[j], dn_norm_g[j], dn_w_out[j], not last)
        else:
            lambda_init = 0.8 - 0.6 * math.exp(-0.3 * i)
            m_ctx, m_lat = diff_attn_mixer(a_ctx, a_lat, da_w_qkv[j], da_q_norm_g[j], da_k_norm_g[j],
                                           da_lambda[j], da_subln_g[j], da_w_out[j],
                                           lambda_init, cos, sin, not last)
        h_lat = h_lat + gt1 * m_lat
        f_lat = modulate(rms_norm(h_lat, norm2_g[i]), sh2, sc2)
        if last:
            y = peer_ffn(f_lat.reshape(-1, dm), peer_wq[i], peer_keys[i], peer_u[i], peer_v[i])
            h_lat = h_lat + gt2 * y.reshape(h_lat.shape)
        else:
            h_ctx = h_ctx + cgt1 * m_ctx
            f_ctx = modulate(rms_norm(h_ctx, norm2_g[i]), csh2, csc2)
            tok = jnp.concatenate([f_ctx, f_lat], axis=1)
            y = peer_ffn(tok.reshape(-1, dm), peer_wq[i], peer_keys[i], peer_u[i], peer_v[i])
            y = y.reshape(tok.shape)
            h_ctx = h_ctx + cgt2 * y[:, :n_ctx]
            h_lat = h_lat + gt2 * y[:, n_ctx:]
    return h_lat


_drawn_inputs = setup_inputs


def setup_inputs(seed=0):
    import zlib

    import numpy as np

    out = dict(_drawn_inputs(seed))
    spreads = {}
    factors = {'norm1_g': 4.587,
     'norm2_g': 11.588,
     'dn_norm_g': 6.214,
     'da_q_norm_g': 8.0,
     'da_k_norm_g': 8.0,
     'da_lambda': 7.366,
     'da_subln_g': 64.0}
    for name, (base, spread) in spreads.items():
        noise = np.random.default_rng([zlib.crc32(name.encode()), seed]).standard_normal(out[name].shape)
        drawn = base * np.exp(spread * noise) if base else spread * noise
        out[name] = jnp.asarray(drawn.astype(out[name].dtype))
    for name, factor in factors.items():
        out[name] = (out[name] * factor).astype(out[name].dtype)
    return out
```

```python
from contextlib import ExitStack
import math

import numpy as np
import concourse.bass as bass
from concourse import mybir

F32 = mybir.dt.float32
U32 = mybir.dt.uint32
ALU = mybir.AluOpType
ACT = mybir.ActivationFunctionType
AX = mybir.AxisListType
ds = bass.ds

D = 1024
KC = D // 128
CTX, LAT = 256, 512
T = CTX + LAT
HEADS = 8
EPS = 1e-6
NCH = T // 128
NG = 16
TOPK = 16
LAMBDA_INIT = 0.8 - 0.6 * math.exp(-0.3)
ALL = [(0, CTX), (CTX, LAT)]
ONLY_LAT = [(CTX, LAT)]
STOP = 99
SKIP_DELTA = 0

O_ADA, O_DN, O_DNOUT, O_WQ0, O_UV0, O_QKV, O_DAOUT, O_WQ1, O_UV1, O_END = (
    0, 12, 16, 17, 19, 51, 54, 55, 57, 89)


def const_table():
    i, j = np.arange(128)[:, None], np.arange(128)[None, :]
    parts = {"ident": i == j, "ones": np.ones((128, 128)), "mean1024": np.full((128, 128), 1 / 1024),
             "mean128": np.full((128, 128), 1 / 128), "mean64": (i // 64 == j // 64) / 64.0,
             "until0": i <= j, "until1": i >= j}
    for n in range(7):
        b = 1 << n
        m = (i // (2 * b) == j // (2 * b)) & ((i // b) % 2 == 1) & ((j // b) % 2 == 0)
        parts[f"level0_{n}"], parts[f"level1_{n}"] = m, m.T
    same = i // 64 == j // 64
    parts["rotate"] = (np.where(same & (i % 64 == j % 64 + 32), -1.0, 0)
                       + np.where(same & (i % 64 == j % 64 - 32), 1.0, 0))
    parts["iota"] = np.broadcast_to(np.arange(128), (128, 128))
    where, at, cols = {}, 0, []
    for name, a in parts.items():
        where[name] = at
        at += a.shape[1]
        cols.append(np.asarray(a, np.float32))
    return where, np.ascontiguousarray(np.concatenate(cols, 1))


def rope_table():
    inv = (np.float32(10000.0) ** (-np.arange(16, dtype=np.float32) / np.float32(16))).astype(np.float32)
    tok = np.arange(LAT)
    row, col = (tok // 64).astype(np.float32), (tok % 64).astype(np.float32)
    ang = np.concatenate([row[:, None] * inv, col[:, None] * inv], 1).astype(np.float32)
    return np.ascontiguousarray(np.stack([np.tile(np.cos(ang).T, (4, 1)), np.tile(np.sin(ang).T, (4, 1))], 1))


def backbone(nc, io, where):
    with ExitStack() as ctx:
        def sb(name, shape, dt=F32):
            return ctx.enter_context(nc.sbuf_tensor(name, shape, dt))

        sems = {}

        def sem(name):
            if name not in sems:
                sems[name] = ctx.enter_context(nc.semaphore(name))
            return sems[name]

        NCONST = max(where.values()) + 128
        const = sb("const", [128, NCONST])

        def C(name):
            return const[:, where[name]:where[name] + 128]

        ring = sb("ring", [128, 8, KC, 128])
        hT = sb("hT", [128, KC, T])
        aT = sb("aT", [128, KC, T])
        ARENA = 42 * T
        arena = sb("arena", [128, ARENA])
        mod = sb("mod", [128, 96, 2])
        gates = sb("gates", [128, 6, NCH, 16])
        small = sb("small", [128, 512])
        lin = ctx.enter_context(nc.psum_tensor("lin", [128, 4, 512], F32))
        aux = ctx.enter_context(nc.psum_tensor("aux", [128, 4, 512], F32))

        taken = [0]

        def sm(w):
            taken[0] += w
            assert taken[0] <= 512
            return small[:, taken[0] - w:taken[0]]

        params = sm(16 + 96 + 32 + 4 + 120 + 32)
        cond = params[:, 0:16].rearrange("p (k c) -> p k c", c=2)
        ada_b = params[:, 16:112]
        norm_g = params[:, 112:144]
        dn_g, da_qg, da_kg, da_sg = (params[:, 144 + n:145 + n] for n in range(4))
        conv_w = params[:, 148:268]
        dt_bias = params[:, 268:284]
        a_log = params[:, 284:300]
        gsc = sm(64).rearrange("p (q k c) -> p q k c", q=4, c=2)
        eps = sm(1)
        lam = sm(8)
        mx = sm(32)

        def Rg(a, w):
            assert a + w <= ARENA
            return arena[:, a:a + w]

        qkvT = Rg(0, 24 * T).rearrange("p (t n) -> p t n", n=T)
        zT = Rg(24 * T, 8 * T).rearrange("p (t n) -> p t n", n=T)
        SCR = 32 * T
        XPW = T + 8
        xp = [Rg(SCR + b * XPW, XPW) for b in range(2)]
        co = [Rg(SCR + (2 + b) * XPW, XPW) for b in range(2)]
        wab = Rg(SCR + 4 * XPW, 32 * KC).rearrange("p (k n) -> p k n", k=KC)
        nrt = [Rg(SCR + 4 * XPW + 32 * KC + 4 * 96 + 2 * T, T)]
        HN = SCR + 4 * XPW + 32 * KC + 4 * 96
        sq = [Rg(HN + b * T, T) for b in range(2)]
        rt = [Rg(HN + (2 + b) * T, T) for b in range(2)]
        gtmp = Rg(SCR + 4 * XPW + 32 * KC, 4 * 96)
        beta, g_, negG, negE, kdf, dec = (gates[:, n, :, :] for n in range(6))

        hflat = hT[:, :, :].rearrange("p k n -> p (k n)")
        blocks = [Rg(SCR + 512 * n, 512) for n in range((ARENA - SCR) // 512)] + \
                 [hflat[:, 512 * n:512 * n + 512] for n in range(KC * T // 512)]

        def four(x):
            return x.rearrange("p (h n) -> p h n", n=128)

        blk = [four(x) for x in blocks]
        (kts, vts, gby, vt, egq, Em, eb, AT, Tm, Um, dl) = ([blk[2 * n + d] for d in range(2)] for n in range(11))
        state = [blk[22 + n] for n in range(4)]

        pqT = Rg(0, 16 * T).rearrange("p (m n) -> p m n", n=T)
        K0 = 16 * T
        keys = Rg(K0, 2048).rearrange("p (m n) -> p m n", n=128)
        qs = Rg(K0 + 2048, 2048).rearrange("p (m n) -> p m n", n=128)
        sc = Rg(K0 + 4096, 2048).rearrange("p (m n) -> p m n", n=128)
        sc2 = Rg(K0 + 6144, 2048).rearrange("p (m n) -> p m n", n=128)
        cand = Rg(K0 + 8192, 2048).rearrange("p (m n) -> p m n", n=256)
        cand2 = Rg(K0 + 10240, 2048).rearrange("p (m n) -> p m n", n=256)
        eq = Rg(K0 + 12288, 2048)
        sp_ = [Rg(K0 + 14336 + 128 * n, 128) for n in range(16)]
        tv = Rg(K0 + 14336, 256).rearrange("p (m n) -> p m n", n=16)
        ti = Rg(K0 + 14336 + 256, 256).bitcast(U32).rearrange("p (m n) -> p m n", n=16)
        tf = Rg(K0 + 14336 + 512, 256).rearrange("p (m n) -> p m n", n=16)
        best = sp_[6].rearrange("p (m n) -> p m n", n=16)
        bpos = sp_[7].bitcast(U32).rearrange("p (m n) -> p m n", n=16)
        posi = [sp_[8].bitcast(U32), sp_[9].bitcast(U32)]
        posf = [sp_[10], sp_[11]]
        chosen = [sp_[12], sp_[13], sp_[14]]
        gsum = sp_[15]
        IDX = K0 + 14336 + 2048
        idx = Rg(IDX, 3 * T).rearrange("p (k n) -> p k n", n=T)
        TB = 32
        stage = [Rg(b * 128 * TB, 128 * TB) for b in range(2)]
        GB = 2 * 128 * TB
        hot = [Rg(GB + 2048 * n, 2048).rearrange("p (m n) -> p m n", n=128) for n in range(2)]
        bidx = [Rg(GB + 4096 + 96 * b, 96).rearrange("p (k n) -> p k n", k=3) for b in range(2)]
        gate_dram = nc.dram_tensor("gate_matrix", (NG, 128, T * 8), F32).ap()
        prod = [Rg(b * 8 * T, 8 * T).rearrange("p (c n) -> p c n", n=T) for b in range(2)]
        ggate = [Rg((16 + 8 * b) * T, 8 * T).rearrange("p (n c) -> p n c", c=8) for b in range(2)]
        acc = Rg(32 * T, 8 * T).rearrange("p (c n) -> p c n", n=T)
        gl = [Rg((40 + b) * T, T) for b in range(2)]
        qT = Rg(0, 8 * T).rearrange("p (c n) -> p c n", n=T)
        kT = Rg(8 * T, 8 * T).rearrange("p (c n) -> p c n", n=T)
        vtok = Rg(16 * T, 8 * T).rearrange("p (c n) -> p c n", n=D)
        A0 = 24 * T
        qst = Rg(A0, D).rearrange("p (c n) -> p c n", n=128)
        pr = [[Rg(A0 + D + (2 * b + c) * T, T) for c in range(2)] for b in range(2)]
        wtt = [Rg(A0 + D + 4 * T, T).rearrange("p (c n) -> p c n", n=128)] * 2
        lamv = Rg(A0 + D + 5 * T, 256).rearrange("p (a b n) -> p a b n", a=2, b=2)
        rope = Rg(A0 + D + 5 * T + 256, 2 * LAT).rearrange("p (a n) -> p a n", a=2)
        rtmp = [[Rg(A0 + D + (2 * b + c) * T, LAT) for c in range(2)] for b in range(2)]
        assert A0 + D + 5 * T + 256 + 2 * LAT <= ARENA
        sqa, rta = [pr[0][0], pr[0][1]], [pr[1][0], pr[1][1]]

        w_ready = [sem(f"weight_ready{i}") for i in range(8)]
        tile_done, lin_free = sem("tile_done"), sem("lin_free")

        class Steps:

            def __init__(self, eng, name):
                self.eng, self.sem, self.n = eng, sem(name), 0

            def mark(self, ins):
                ins.then_inc(self.sem, 1)
                self.n += 1

            def wait(self):
                self.eng.wait_ge(self.sem, self.n)

            def __call__(self, ins):
                self.mark(ins)
                self.wait()

            def restart(self):
                self.eng.sem_clear(self.sem)
                self.n = 0

        def heads4(x):
            return x.unsqueeze(1).to_broadcast([128, 4, 128])

        def cols(x, n=128):
            return x.unsqueeze(2).to_broadcast([128, x.shape[1], n])

        block = ctx.enter_context(nc.Block())

        @block.sync
        def _(sp):
            sp.dma_start(params, io["params"]).then_inc(sem("params_ready"), 16)
            sp.dma_start(const[:, :], io["const"]).then_inc(sem("const_ready"), 16)
            for i in range(8):
                sp.dma_start(ring[:, i, :, :], io["weights"][i]).then_inc(w_ready[i], 16)
            sp.dma_start(hT[:, :, :], io["x"]).then_inc(sem("x_ready"), 16)
            sp.dma_start(wab, io["w_ab"]).then_inc(sem("wab_ready"), 16)
            with sp.Fori(1, LAST_OCTET) as o:
                for i in range(8):
                    sp.wait_ge(tile_done, o * 8 + (i - 7))
                    sp.dma_start(ring[:, i, :, :], io["weights"][ds(o * 8 + i, 1), :, :, :].rearrange("o p k n -> (o p) k n"))\
                        .then_inc(w_ready[i], 16)
            if STOP > 50:
                sp.wait_ge(sem("h_done"), H_END)
                sp.dma_start(io["out"], hT[:, :, CTX:T]).then_inc(sem("out_done"), 16)
                sp.wait_ge(sem("out_done"), 16)

        @block.tensor
        def _(pe):
            def octet(o, tile):
                for i in range(8):
                    pe.wait_ge(w_ready[i], o * 16 + 16)
                    tile(i).then_inc(tile_done, 1)

            def lin_octet(o, rhs, segs=ALL):
                def tile(i):
                    pe.wait_ge(lin_free, o * 8 + (i + 1 - 8 * O_DN))
                    for k, (a, w) in enumerate(segs):
                        for kc in range(KC):
                            last = nc.tensor.matmul(lin[:, 2 * (i % 2) + k, 0:w], ring[:, i, kc, :],
                                                    rhs(kc)[:, a:a + w], start=kc == 0, stop=kc == KC - 1)
                    return last
                octet(o, tile)

            def norm(q, segs):
                for kc in range(KC):
                    pe.wait_ge(sem("norm_sq"), 8 * q + kc + 1)
                    for k, (a, w) in enumerate(segs):
                        last = nc.tensor.matmul(aux[:, k, 0:w], C("mean1024"), aT[:, kc, a:a + w],
                                                start=kc == 0, stop=kc == KC - 1)
                last.then_inc(sem("norm_sum"), 1)

            def peer(L, segs):
                o_wq, o_uv, nt, u0 = (O_WQ0, O_UV0, NCH, 0) if L == 0 else (O_WQ1, O_UV1, LAT // 128, NCH)
                pe.wait_ge(sem("norm_done"), 16 * (2 * L + 2))
                with pe.Fori(o_wq, o_wq + 2) as o:
                    lin_octet(o, lambda kc: aT[:, kc, :], segs)
                pe.wait_ge(sem("keys_ready"), 16 * (L + 1))
                with pe.Fori(0, nt) as n:
                    pe.wait_ge(sem("tk_query"), n + (u0 + 1))
                    for m in range(16):
                        last = nc.tensor.matmul(aux[:, m // 4, 128 * (m % 4):128 * (m % 4) + 128], qs[:, m, :],
                                                keys[:, m, :], start=True, stop=True)
                    last.then_inc(sem("tk_scores"), 1)
                    pe.wait_ge(sem("tk_chosen"), n + (u0 + 1))
                    for k in range(3):
                        last = nc.tensor.transpose(lin[:, 0, 128 * k:128 * k + 128], chosen[k], C("ident"))
                    last.then_inc(sem("tk_turned"), 1)
                if STOP <= 5:
                    return
                q0 = 32 * u0
                with pe.Fori(0, 2 * nt) as n:
                    for q in range(16):
                        pe.wait_ge(sem("gb_hot"), n * 16 + (q0 + q + 1))
                        pe.wait_ge(sem("gb_kept"), n * 16 + (q0 + q + 1))
                        bank = (lin if q % 8 < 4 else aux)[:, q % 4, :]
                        for t in range(4):
                            k = 4 * (q % 4) + t
                            last = nc.tensor.matmul(bank[:, 128 * t:128 * t + 128], hot[0][:, k, :], hot[1][:, k, :],
                                                    start=True, stop=True)
                        last.then_inc(sem("gb_sum"), 1)
                if STOP <= 6:
                    return
                pe.wait_ge(sem("gb_kept"), 8 + q0 + 32 * nt)

                def v_octet(o, g, b):
                    pe.wait_ge(sem("p_done"), g * 8 + (10 + 128 * L))
                    def tile(i):
                        pe.wait_ge(lin_free, o * 8 + (i + 1 - 8 * O_DN))
                        for k, (a, w) in enumerate(segs):
                            for c in range(8):
                                last = nc.tensor.matmul(lin[:, 2 * (i % 2) + k, 0:w], ring[:, i, c, :],
                                                        prod[b][:, c, a:a + w], start=c == 0, stop=c == 7)
                        return last
                    octet(o, tile)

                f = lambda kc: aT[:, kc, :]
                lin_octet(o_uv, f, segs)
                with pe.Fori(0, 7) as n:
                    o = n * 4 + o_uv
                    lin_octet(o + 1, f, segs)
                    v_octet(o + 2, n * 2, 0)
                    lin_octet(o + 3, f, segs)
                    v_octet(o + 4, n * 2 + 1, 1)
                lin_octet(o_uv + 29, f, segs)
                v_octet(o_uv + 30, 14, 0)
                v_octet(o_uv + 31, 15, 1)

            def head_norm(base, iters, ones, segs, sq=sq):
                with pe.Fori(0, iters) as n:
                    for b in range(2):
                        pe.wait_ge(sem("hn_sq"), n * 2 + (base + b + 1))
                        pe.wait_ge(sem("hn_root"), n * 2 + (base + b + 1))
                        for k, (a, w) in enumerate(segs):
                            last = nc.tensor.matmul(aux[:, 2 * b + k, 0:w], ones, sq[b][:, a:a + w],
                                                    start=True, stop=True)
                        last.then_inc(sem("hn_sum"), 1)

            pe.wait_ge(sem("cond_ready"), 1)
            with pe.Fori(O_ADA, O_DN) as o:
                def ada(i):
                    for kc in range(KC):
                        last = nc.tensor.matmul(aux[:, 0, ds(o * 16 + 2 * i, 2)], ring[:, i, kc, :],
                                                cond[:, kc, :], start=kc == 0, stop=kc == KC - 1)
                    return last
                octet(o, ada)
            pe.wait_ge(sem("ada_read"), 1)
            pe.wait_ge(sem("const_ready"), 16)
            norm(0, ALL)

            pe.wait_ge(sem("norm_done"), 16)
            pe.wait_ge(sem("wab_ready"), 16)
            for t in range(NCH):
                for kc in range(KC):
                    last = nc.tensor.matmul(aux[:, 2, 32 * t:32 * t + 32], aT[:, kc, 128 * t:128 * t + 128],
                                            wab[:, kc, :], start=kc == 0, stop=kc == KC - 1)
            last.then_inc(sem("gate_sum"), 1)
            pe.wait_ge(sem("norm_done"), 16)
            with pe.Fori(O_DN, O_DN + 3) as o:
                lin_octet(o, lambda kc: aT[:, kc, :])
            lin_octet(O_DN + 3, lambda kc: aT[:, kc, :])
            if STOP <= 1:
                return
            pe.wait_ge(sem("gate_ready"), 1)
            for d in range(2):
                nc.tensor.matmul(aux[:, 3, 0:96].rearrange("p (c n) -> p c n", n=16)[:, :, 8 * d:8 * d + 8],
                                 C(f"until{d}"), g_[:, :, 8 * d:8 * d + 8], start=True, stop=True)
            nc.tensor.matmul(aux[:, 3, 128:224], C("ones"), g_.rearrange("p c n -> p (c n)"),
                             start=True, stop=True).then_inc(sem("gate_tot"), 1)
            pe.wait_ge(sem("gates_done"), 1)
            head_norm(0, 8, C("ones"), ALL)
            if STOP <= 2:
                return

            P = [[lin[:, 2 * d + k, :].rearrange("p (h n) -> p h n", n=128) for k in range(2)] for d in range(2)]

            def each(out, lhs, rhs, start=True, stop=True, op=None):
                for h in range(4):
                    last = nc.tensor.matmul(out[:, h, :], lhs(h), rhs(h), start=start, stop=stop)
                return last

            def delta(n, chunk):
                for hg in range(2):
                    use = [[0, 0], [0, 0]]

                    def bank(d, k):
                        pe.wait_ge(sem(f"bank_read{d}{k}"), n * (2 * USES[k]) + hg * USES[k] + use[d][k] + DB(k))
                        use[d][k] += 1
                        return P[d][k]

                    def full(d, k, last):
                        last.then_inc(sem(f"bank_full{d}{k}"), 1)

                    for d in range(2):
                        pe.wait_ge(sem(f"staged{d}"), n * 4 + 2 * hg + 1)
                        full(d, 0, each(bank(d, 0), lambda h: gby[d][:, h, :], lambda h: C(f"until{d}")))
                    for d in range(2):
                        pe.wait_ge(sem(f"staged{d}"), n * 4 + 2 * hg + 2)
                        full(d, 1, each(bank(d, 1), lambda h: kts[d][:, h, :], lambda h: kts[d][:, h, :]))
                    for d in range(2):
                        out = bank(d, 0)
                        for h in range(4):
                            last = nc.tensor.transpose(out[:, h, :], vts[d][:, h, :], C("ident"))
                        full(d, 0, last)
                    for d in range(2):
                        full(d, 1, each(bank(d, 1), lambda h: kts[d][:, h, :],
                                        lambda h: qkvT[:, 4 * hg + h, ds(chunk[d] * 128, 128)]))
                    for d in range(2):
                        full(d, 0, each(bank(d, 0), lambda h: AT[d][:, h, :], lambda h: C("ident")))
                    for lv in range(1, 7):
                        for d in range(2):
                            pe.wait_ge(sem(f"inverse{d}"), n * 14 + 7 * hg + lv + 0)
                            full(d, 0, each(bank(d, 0), lambda h: AT[d][:, h, :], lambda h: Tm[d][:, h, :]))
                        for d in range(2):
                            out1, out0 = bank(d, 1), bank(d, 0)
                            if lv < 6:
                                full(d, 1, each(out1, lambda h: Um[d][:, h, :], lambda h: gby[d][:, h, :]))
                            full(d, 0, each(out0, lambda h: gby[d][:, h, :], lambda h: Um[d][:, h, :]))
                            if lv == 6:
                                use[d][1] -= 1
                    for d in range(2):
                        pe.wait_ge(sem(f"state_ready{d}"), n * 2 + hg + 1)
                        full(d, 1, each(bank(d, 1), lambda h: kts[d][:, h, :], lambda h: state[2 * hg + d][:, h, :]))
                    for d in range(2):
                        out = bank(d, 0)
                        for h in range(4):
                            last = nc.tensor.transpose(out[:, h, :], kts[d][:, h, :], C("ident"))
                        full(d, 0, last)
                    for d in range(2):
                        pe.wait_ge(sem(f"inverse{d}"), n * 14 + 7 * hg + 7)
                        out = bank(d, 1)
                        full(d, 1, each(out, lambda h: Um[d][:, h, :], lambda h: eb[d][:, h, :]))
                    for d in range(2):
                        pe.wait_ge(sem(f"q_decayed{d}"), n * 2 + hg + 1)
                        out0, out1 = bank(d, 0), bank(d, 1)
                        for h in range(4):
                            nc.tensor.matmul(out0[:, h, :], state[2 * hg + d][:, h, :], egq[d][:, h, :],
                                             start=True, stop=False)
                            last = nc.tensor.matmul(out0[:, h, :], dl[d][:, h, :], Em[d][:, h, :],
                                                    start=False, stop=True)
                        full(d, 0, last)
                        full(d, 1, each(out1, lambda h: kts[d][:, h, :], lambda h: dl[d][:, h, :]))

            if not SKIP_DELTA:
                with pe.Fori(0, 2) as n:
                    delta(n, [n, pe.snap(n * (-1) + 1)])
                with pe.Fori(2, NCH) as n:
                    delta(n, [n, pe.snap(n * (-1) + 7)])
            if STOP <= 3:
                return
            pe.wait_ge(sem("delta_done"), 1)
            head_norm(16, 4, C("mean128"), ALL)
            pe.wait_ge(sem("hn_out"), 2 + 24)
            lin_octet(O_DNOUT, lambda kc: aT[:, kc, :])
            if STOP <= 4:
                return
            norm(1, ALL)
            peer(0, ALL)
            if STOP <= 7:
                return
            norm(2, ALL)

            pe.wait_ge(sem("norm_done"), 48)
            lin_octet(O_QKV, lambda kc: aT[:, kc, :], ONLY_LAT)
            lin_octet(O_QKV + 1, lambda kc: aT[:, kc, :])

            def v_tile(i):
                pe.wait_ge(lin_free, 8 * (O_QKV + 2 - O_DN) + i + 1)
                for t in range(NCH):
                    for kc in range(KC):
                        last = nc.tensor.matmul(lin[:, 2 * (i % 2) + t // 3, (t % 3) * 128:(t % 3) * 128 + 128],
                                                aT[:, kc, 128 * t:128 * t + 128], ring[:, i, kc, :],
                                                start=kc == 0, stop=kc == KC - 1)
                return last
            octet(O_QKV + 2, v_tile)
            head_norm(24, 4, C("mean64"), ONLY_LAT, sqa)
            head_norm(32, 4, C("mean64"), ALL, sqa)
            pe.wait_ge(sem("hn_out"), 2 + 40)
            with pe.Fori(0, 8) as n:
                for b in range(2):
                    pe.wait_ge(sem("rope_done"), n * 2 + (b + 1))
                    x = (kT if b else qT)[:, ds(n, 1), CTX:T].rearrange("p o n -> p (o n)")
                    nc.tensor.matmul(aux[:, b, :], C("rotate"), x, start=True, stop=True)\
                        .then_inc(sem("rope_turned"), 1)
            pe.wait_ge(sem("rope_done"), 18)
            with pe.Fori(0, LAT // 128) as n:
                pe.wait_ge(sem("at_query"), n + 1)

                def scores(h):
                    pe.wait_ge(sem("at_exp"), n * 8 + (h + 1))
                    for c in range(2):
                        for k in range(2):
                            last = nc.tensor.matmul(aux[:, 2 * c + k, 0:T // 2], qst[64 * c:64 * c + 64, h, :],
                                                    kT[64 * c:64 * c + 64, h, k * T // 2:(k + 1) * T // 2],
                                                    start=True, stop=True)
                    last.then_inc(sem("at_scores"), 1)
                scores(0)
                for h in range(8):
                    if h < 7:
                        scores(h + 1)
                    pe.wait_ge(sem("at_weights"), n * 8 + (h + 1))
                    pe.wait_ge(sem("at_turned"), n * 8 + (h + 1))
                    for j in range(NCH):
                        last = nc.tensor.transpose(lin[:, j // 3, (j % 3) * 128:(j % 3) * 128 + 128],
                                                   pr[h % 2][0][:, 128 * j:128 * j + 128], C("ident"))
                    last.then_inc(sem("at_turn"), 1)
                    pe.wait_ge(sem("at_turned"), n * 8 + (h + 2))
                    pe.wait_ge(sem("at_kept"), n * 8 + (h + 1))
                    for j in range(NCH):
                        last = nc.tensor.matmul(lin[:, 2, 0:128], vtok[:, j, 128 * h:128 * h + 128], wtt[h % 2][:, j, :],
                                                start=j == 0, stop=j == NCH - 1)
                    last.then_inc(sem("at_out"), 1)
            head_norm(40, 4, C("mean128"), ONLY_LAT, sqa)
            pe.wait_ge(sem("hn_out"), 2 + 48)
            lin_octet(O_DAOUT, lambda kc: aT[:, kc, :], ONLY_LAT)
            if STOP <= 8:
                return
            norm(3, ONLY_LAT)
            peer(1, ONLY_LAT)

        @block.scalar
        def _(act):
            step = Steps(act, "act_step")

            def norm(q, segs, h_count):
                t0 = segs[0][0]
                rt = nrt
                if h_count:
                    act.wait_ge(sem("h_done"), h_count)
                for kc in range(KC):
                    nc.scalar.activation(aT[:, kc, t0:T], hT[:, kc, t0:T], ACT.Square).then_inc(sem("norm_sq"), 1)
                act.wait_ge(sem("norm_sum"), q + 1)
                for k, (a, w) in enumerate(segs):
                    last = nc.scalar.activation(rt[0][:, a:a + w], aux[:, k, 0:w], ACT.Ln, bias=eps)
                step(last)
                nc.scalar.activation(rt[0][:, t0:T], rt[0][:, t0:T], ACT.Exp, scale=-0.5).then_inc(sem("norm_root"), 1)
                for kc in range(KC):
                    act.wait_ge(sem("norm_scaled"), 8 * q + kc + 1)
                    for k, (a, w) in enumerate(segs):
                        c = 0 if a == CTX else 1
                        ins = nc.scalar.activation(aT[:, kc, a:a + w], aT[:, kc, a:a + w], ACT.Identity,
                                                   bias=mod[:, 48 * (q // 2) + 24 * (q % 2) + kc, c:c + 1])
                        ins.then_inc(sem("norm_done"), 2 // len(segs))

            def copy_octets(o0, n, to, segs):
                with act.Fori(0, n) as m:
                    for i in range(8):
                        act.wait_ge(tile_done, m * 8 + (8 * o0 + i + 1))
                        for k, (a, w) in enumerate(segs):
                            last = nc.scalar.copy(to(m, i)[:, :, a:a + w], lin[:, 2 * (i % 2) + k, 0:w].unsqueeze(1))
                        last.then_inc(lin_free, 1)

            def peer(L, segs):
                o_wq, o_uv, nt, u0 = (O_WQ0, O_UV0, NCH, 0) if L == 0 else (O_WQ1, O_UV1, LAT // 128, NCH)
                t0 = segs[0][0]
                act.dma_start(keys, io["keys"][L]).then_inc(sem("keys_ready"), 16)
                copy_octets(o_wq, 2, lambda m, i: pqT[:, ds(m * 8 + i, 1), :], segs)
                act.wait_ge(lin_free, 8 * (o_wq + 2 - O_DN) + 2)
                with act.Fori(0, nt) as n:
                    step.restart()
                    nc.scalar.copy(qs, pqT[:, :, ds(n * 128 + t0, 128)]).then_inc(sem("tk_query"), 1)
                    act.wait_ge(sem("tk_scores"), n + (u0 + 1))
                    nc.scalar.copy(sc.rearrange("p m n -> p (m n)"), aux[:, :, :].rearrange("p b n -> p (b n)"))\
                        .then_inc(sem("tk_kept"), 1)
                    act.wait_ge(sem("tk_shifted"), n + (u0 + 1))
                    nc.scalar.activation(chosen[2], chosen[2], ACT.Exp).then_inc(sem("tk_exp"), 1)
                    act.wait_ge(sem("tk_turned"), n + (u0 + 1))
                    step(nc.scalar.copy(idx[:, :, ds(n * 128, 128)], lin[:, 0, 0:384].rearrange("p (k n) -> p k n", k=3)))
                step.restart()
                act.sem_inc(sem("idx_ready"), 1)
                if STOP <= 5:
                    return
                q0 = 32 * u0
                with act.Fori(0, 2 * nt) as n:
                    for b in range(2):
                        act.wait_ge(sem(f"gb_stored{b}"), n * 16 + 16 * (2 * u0 + 1))
                        out = stage[b].rearrange("p (g t c) -> p t g c", g=NG, c=8)
                        for q in range(8):
                            act.wait_ge(sem("gb_sum"), n * 16 + (q0 + 8 * b + q + 5))
                            bank = (lin if q % 8 < 4 else aux)[:, q % 4, :]
                            nc.scalar.copy(out[:, 4 * q:4 * q + 4, :, :], bank.rearrange("p (t g c) -> p t g c", t=4, c=8))\
                                .then_inc(sem("gb_kept"), 1)
                        act.wait_ge(sem("gb_kept"), n * 16 + (q0 + 8 * b + 16))
                        act.dma_start(gate_dram[:, :, ds(n * 512 + (256 * b + 8 * t0), 256)].rearrange("g p x -> p g x"),
                                      stage[b].rearrange("p (g x) -> p g x", g=NG)).then_inc(sem(f"gb_stored{b}"), 16)
                if STOP <= 6:
                    for b in range(2):
                        act.wait_ge(sem(f"gb_stored{b}"), 16 * (2 * (u0 + nt) + 1))
                    return
                for b in range(2):
                    act.wait_ge(sem(f"gb_stored{b}"), 16 * (2 * (u0 + nt) + 1))
                act.wait_ge(sem("gb_sum"), 4 + q0 + 32 * nt)

                def load(g, b):
                    act.dma_start(ggate[b][:, t0:T, :].rearrange("p n c -> p (n c)"),
                                  gate_dram[ds(g, 1), :, 8 * t0:8 * T].rearrange("o p x -> (o p) x"))\
                        .then_inc(sem(f"gg_ready{b}"), 16)

                def gelu_octet(o, g):
                    act.wait_ge(lin_free, o * 8 + (2 - 8 * O_DN))
                    for i in range(8):
                        act.wait_ge(tile_done, o * 8 + (i + 1))
                        act.wait_ge(sem("p_done"), g * 8 + (i + 1 + 128 * L))
                        for k, (a, w) in enumerate(segs):
                            last = nc.scalar.activation(gl[i % 2][:, a:a + w], lin[:, 2 * (i % 2) + k, 0:w], ACT.Gelu)
                        last.then_inc(lin_free, 1)

                def reload(g, b):
                    act.wait_ge(sem("p_done"), g * 8 + (128 * L - 6))
                    load(g, b)

                load(0, 0)
                load(1, 1)
                gelu_octet(o_uv, 0)
                with act.Fori(0, 7) as n:
                    for b in range(2):
                        reload(n * 2 + (b + 2), b)
                        gelu_octet(n * 4 + (o_uv + 1 + 2 * b), n * 2 + (b + 1))
                gelu_octet(o_uv + 29, 15)

            def head_norm(base, iters, src, segs, e, sq=sq, rt=rt):
                t0 = segs[0][0]
                with act.Fori(0, iters) as n:
                    step.restart()
                    for b in range(2):
                        act.wait_ge(sem("hn_sum"), n * 2 + (base + b + 1))
                        nc.scalar.activation(sq[b][:, t0:T], src(n, b)[:, t0:T], ACT.Square).then_inc(sem("hn_sq"), 1)
                    for b in range(2):
                        act.wait_ge(sem("hn_sum"), n * 2 + (base + b + 3))
                        act.wait_ge(sem("hn_out"), n * 2 + (base + b + 1))
                        for k, (a, w) in enumerate(segs):
                            last = nc.scalar.activation(rt[b][:, a:a + w], aux[:, 2 * b + k, 0:w], ACT.Ln, bias=e)
                        step(last)
                        nc.scalar.activation(rt[b][:, t0:T], rt[b][:, t0:T], ACT.Exp, scale=-0.5).then_inc(sem("hn_root"), 1)

            act.sem_inc(lin_free, 2)
            for x in ("conv_done", "silu_done", "hn_sum", "hn_root", "hn_out"):
                act.sem_inc(sem(x), 2)
            for x in ("rope_done", "p_done"):
                act.sem_inc(sem(x), 2)
            for x in ("at_exp", "at_turned", "at_kept", "at_used"):
                act.sem_inc(sem(x), 1)
            act.sem_inc(sem("gb_kept"), 8)
            act.sem_inc(sem("gb_sum"), 4)
            for b in range(2):
                act.sem_inc(sem(f"gb_stored{b}"), 16)
            for x in ("bank_read00", "bank_read01", "bank_read10", "bank_read11"):
                act.sem_inc(sem(x), 1)
            act.wait_ge(sem("params_ready"), 16)
            nc.scalar.activation(cond, cond, ACT.Silu).then_inc(sem("cond_ready"), 1)
            act.wait_ge(sem("x_ready"), 16)
            act.wait_ge(sem("pads_ready"), 2)
            act.wait_ge(sem("mod_ready"), 1)
            norm(0, ALL, 0)

            with act.Fori(0, 3) as n:
                def silu(i):
                    b = i % 2
                    act.wait_ge(sem("conv_done"), n * 8 + (i + 3))
                    nc.scalar.activation(qkvT[:, ds(n * 8 + i, 1), 0:CTX], co[b][:, 0:CTX].unsqueeze(1), ACT.Silu)
                    nc.scalar.activation(qkvT[:, ds(n * 8 + i, 1), CTX:T], co[b][:, CTX + 4:T + 4].unsqueeze(1), ACT.Silu)\
                        .then_inc(sem("silu_done"), 1)
                for i in range(8):
                    b = i % 2
                    act.wait_ge(tile_done, n * 8 + (8 * O_DN + i + 1))
                    act.wait_ge(sem("conv_done"), n * 8 + (i + 1))
                    nc.scalar.copy(xp[b][:, 2:2 + CTX], lin[:, 2 * b, 0:CTX])
                    nc.scalar.copy(xp[b][:, 6 + CTX:6 + T], lin[:, 2 * b + 1, :]).then_inc(lin_free, 1)
                    if i:
                        silu(i - 1)
                silu(7)
            for i in range(8):
                act.wait_ge(tile_done, 8 * (O_DN + 3) + i + 1)
                nc.scalar.activation(zT[:, i, 0:CTX], lin[:, 2 * (i % 2), 0:CTX], ACT.Silu)
                nc.scalar.activation(zT[:, i, CTX:T], lin[:, 2 * (i % 2) + 1, :], ACT.Silu).then_inc(lin_free, 1)
            if STOP <= 1:
                return
            act.wait_ge(sem("gate_sum"), 1)
            ab = aux[:, 2, 0:192].rearrange("p (c k n) -> p c k n", c=NCH, k=2)
            nc.scalar.activation(beta, ab[:, :, 0, :], ACT.Sigmoid).then_inc(sem("beta_ready"), 1)
            step(nc.scalar.activation(a_log, a_log, ACT.Exp))
            act.wait_ge(sem("gate_abs"), 1)
            step(nc.scalar.activation(gtmp[:, 96:192], gtmp[:, 96:192], ACT.Exp, scale=-1.0))
            nc.scalar.activation(gtmp[:, 96:192], gtmp[:, 96:192], ACT.Ln, bias=1.0).then_inc(sem("gate_ln"), 1)
            act.wait_ge(sem("gate_tot"), 1)
            act.wait_ge(sem("gate_diff"), 1)
            nc.scalar.activation(kdf, kdf, ACT.Exp)
            nc.scalar.activation(dec.rearrange("p c n -> p (c n)"), aux[:, 3, 128:224], ACT.Exp)
            nc.scalar.activation(negE, negG, ACT.Exp, scale=-1.0).then_inc(sem("gates_exp"), 1)
            act.wait_ge(sem("gates_done"), 1)
            head_norm(0, 8, lambda n, b: qkvT[:, ds(n + 8 * b, 1), :].rearrange("p o n -> p (o n)"), ALL, eps)
            if STOP <= 2:
                return

            def delta(n, chunk):
                for hg in range(2):
                    for d in range(2):
                        act.wait_ge(sem(f"diff_done{d}"), n * 2 + hg + 1)
                        nc.scalar.activation(egq[d], lin[:, 2 * d, :].rearrange("p (h n) -> p h n", n=128), ACT.Exp)\
                            .then_inc(sem(f"bank_read{d}0"), 1)
                    for d in range(2):
                        nc.scalar.activation(Em[d], Em[d], ACT.Exp).then_inc(sem(f"pair_decay{d}"), 1)
                    for d in range(2):
                        act.wait_ge(sem(f"bank_full{d}0"), n * (2 * USES[0]) + hg * USES[0] + 2)
                        nc.scalar.copy(vt[d], lin[:, 2 * d, :].rearrange("p (h n) -> p h n", n=128))\
                            .then_inc(sem(f"bank_read{d}0"), 1)

            if not SKIP_DELTA:
                with act.Fori(0, 2) as n:
                    delta(n, [n, act.snap(n * (-1) + 1)])
                with act.Fori(2, NCH) as n:
                    delta(n, [n, act.snap(n * (-1) + 7)])
            if STOP <= 3:
                return
            act.wait_ge(sem("delta_done"), 1)
            act.dma_start(hT[:, :, :], io["x"]).then_inc(sem("x_ready"), 16)
            head_norm(16, 4, lambda n, b: aT[:, ds(n * 2 + b, 1), :].rearrange("p o n -> p (o n)"), ALL, eps)
            if STOP <= 4:
                return
            step.restart()
            norm(1, ALL, 1)
            act.wait_ge(sem("norm_done"), 32)
            peer(0, ALL)
            if STOP <= 7:
                return
            norm(2, ALL, 2)
            act.dma_start(rope, io["rope"]).then_inc(sem("rope_ready"), 16)
            act.dma_start(lamv.rearrange("p a b n -> p (a b n)"), io["lambdas"]).then_inc(sem("lambdas_ready"), 16)
            copy_octets(O_QKV, 1, lambda m, i: qT[:, i:i + 1, :], ONLY_LAT)
            copy_octets(O_QKV + 1, 1, lambda m, i: kT[:, i:i + 1, :], ALL)
            for i in range(8):
                act.wait_ge(tile_done, 8 * (O_QKV + 2) + i + 1)
                for k in range(2):
                    last = nc.scalar.copy(vtok[:, 3 * k:3 * k + 3, 128 * i:128 * i + 128],
                                          lin[:, 2 * (i % 2) + k, 0:384].rearrange("p (t n) -> p t n", t=3))
                last.then_inc(lin_free, 1)
            act.wait_ge(sem("lam_sums"), 1)
            nc.scalar.activation(lam[:, 0:2], lam[:, 0:2], ACT.Exp).then_inc(sem("lam_exp"), 1)
            act.wait_ge(lin_free, 8 * (O_QKV + 3 - O_DN) + 2)
            one = lambda x, n, b: x[:, ds(n * 2 + b, 1), :].rearrange("p o n -> p (o n)")
            head_norm(24, 4, lambda n, b: one(qT, n, b), ONLY_LAT, eps, sqa, rta)
            head_norm(32, 4, lambda n, b: one(kT, n, b), ALL, eps, sqa, rta)
            with act.Fori(0, LAT // 128) as n:
                def exps(h):
                    act.wait_ge(sem("at_max"), n * 8 + (h + 1))
                    for c in range(2):
                        last = nc.scalar.activation(pr[h % 2][c].rearrange("p (k n) -> p k n", k=2),
                                                    aux[:, 2 * c:2 * c + 2, 0:T // 2], ACT.Exp,
                                                    bias=mx[:, 4 * (h % 2) + 2 + c:4 * (h % 2) + 3 + c],
                                                    accum_out=mx[:, 8 + 4 * (h % 2) + c:9 + 4 * (h % 2) + c])
                    last.then_inc(sem("at_exp"), 1)
                exps(0)
                for h in range(8):
                    act.wait_ge(sem("at_turn"), n * 8 + (h + 1))
                    nc.scalar.copy(wtt[h % 2].rearrange("p (k t) n -> p k (t n)", k=2), lin[:, 0:2, 0:384])\
                        .then_inc(sem("at_turned"), 1)
                    if h < 7:
                        exps(h + 1)
            act.wait_ge(sem("at_kept"), 33)
            head_norm(40, 4, lambda n, b: one(aT, n, b), ONLY_LAT, eps, sqa, rta)
            if STOP <= 8:
                return
            step.restart()
            norm(3, ONLY_LAT, 3)
            act.wait_ge(sem("norm_done"), 64)
            peer(1, ONLY_LAT)

        @block.gpsimd
        def _(pool):
            step = Steps(pool, "pool_step")
            nc.gpsimd.memset(eps, EPS).then_inc(sem("pads_ready"), 1)
            nc.gpsimd.memset(Rg(SCR, 2 * XPW), 0.0).then_inc(sem("pads_ready"), 1)
            if STOP <= 2:
                return
            pool.wait_ge(sem("hn_out"), 2 + 16)
            for x in state:
                nc.gpsimd.memset(x, 0.0).then_inc(sem("state_zero"), 1)
            nc.gpsimd.memset(aT[:, :, :], 0.0).then_inc(sem("o_zero"), 1)

            def delta(n, chunk):
                for hg in range(2):
                    for d in range(2):
                        H = slice(4 * hg, 4 * hg + 4)
                        pool.wait_ge(sem(f"state_ready{d}"), n * 2 + hg + 1)
                        nc.gpsimd.tensor_copy(gby[d], cols(g_[:, ds(chunk[d], 1), 8 * d + 4 * hg:8 * d + 4 * hg + 4]
                                              .rearrange("p o n -> p (o n)"))).then_inc(sem(f"staged{d}"), 1)
                        c = ds(chunk[d] * 128, 128)
                        nc.gpsimd.tensor_copy(kts[d], qkvT[:, 8 + 4 * hg:12 + 4 * hg, c])
                        nc.gpsimd.tensor_copy(vts[d], qkvT[:, 16 + 4 * hg:20 + 4 * hg, c]).then_inc(sem(f"staged{d}"), 1)
                    for d in range(2):
                        pool.wait_ge(sem(f"bank_read{d}0"), n * (2 * USES[0]) + hg * USES[0] + 1 + DB(0))
                        c = ds(chunk[d] * 128, 128)
                        nc.gpsimd.tensor_tensor(egq[d], egq[d], qkvT[:, 4 * hg:4 * hg + 4, c], ALU.mult)\
                            .then_inc(sem(f"q_decayed{d}"), 1)

            if not SKIP_DELTA:
                with pool.Fori(0, 2) as n:
                    delta(n, [n, pool.snap(n * (-1) + 1)])
                with pool.Fori(2, NCH) as n:
                    delta(n, [n, pool.snap(n * (-1) + 7)])
            if STOP <= 6:
                return
            pool.wait_ge(sem("gb_kept"), 8 + 32 * NCH)
            nc.gpsimd.memset(acc, 0.0).then_inc(sem("acc_zero"), 1)
            if STOP <= 7:
                return
            with pool.Fori(0, LAT // 128) as n:
                pool.wait_ge(sem("rope_done"), 18)
                pool.wait_ge(sem("at_used"), n + 1)
                nc.gpsimd.tensor_copy(qst, qT[:, :, ds(n * 128 + CTX, 128)]).then_inc(sem("at_query"), 1)
            if STOP <= 8:
                return
            pool.wait_ge(sem("gb_kept"), 8 + 32 * (NCH + LAT // 128))
            nc.gpsimd.memset(acc, 0.0).then_inc(sem("acc_zero"), 1)

        @block.vector
        def _(dve):
            step = Steps(dve, "dve_step")
            V = nc.vector

            def norm(q, segs):
                t0 = segs[0][0]
                rt = nrt
                dve.wait_ge(sem("norm_root"), q + 1)
                for kc in range(KC):
                    for k, (a, w) in enumerate(segs):
                        c = 0 if a == CTX else 1
                        last = V.scalar_tensor_tensor(aT[:, kc, a:a + w], hT[:, kc, a:a + w], gsc[:, q, kc, c:c + 1],
                                                      rt[0][:, a:a + w], ALU.mult, ALU.mult)
                    last.then_inc(sem("norm_scaled"), 1)

            def head_norm(base, iters, src, segs, gain, gate=None, rt=rt):
                t0 = segs[0][0]
                with dve.Fori(0, iters) as n:
                    step.restart()
                    for b in range(2):
                        dve.wait_ge(sem("hn_root"), n * 2 + (base + b + 3))
                        x = src(n, b)[:, t0:T]
                        ins = V.scalar_tensor_tensor(x, x, gain(b), rt[b][:, t0:T], ALU.mult, ALU.mult)
                        if gate:
                            step(ins)
                            ins = V.tensor_tensor(x, x, gate(n, b)[:, t0:T], ALU.mult)
                        ins.then_inc(sem("hn_out"), 1)
                step.restart()

            dve.wait_ge(tile_done, 96)
            dve.wait_ge(sem("params_ready"), 16)
            V.tensor_tensor(mod[:, :, :], aux[:, 0, 0:192].rearrange("p (t c) -> p t c", c=2), cols(ada_b, 2),
                            ALU.add).then_inc(sem("ada_read"), 1)
            dve.wait_ge(sem("ada_read"), 1)
            for q in range(4):
                a = 48 * (q // 2) + 24 * (q % 2) + 8
                ins = V.scalar_tensor_tensor(gsc[:, q, :, :], mod[:, a:a + 8, :], 1.0, cols(norm_g[:, 8 * q:8 * q + 8], 2),
                                             ALU.add, ALU.mult)
                step(ins)
            dve.sem_inc(sem("mod_ready"), 1)
            norm(0, ALL)

            with dve.Fori(0, 3) as n:
                step.restart()
                for i in range(8):
                    b = i % 2
                    dve.wait_ge(lin_free, n * 8 + (i + 3))
                    dve.wait_ge(sem("silu_done"), n * 8 + (i + 1))
                    w = [conv_w[:, ds(n * 40 + (5 * i + k), 1)] for k in range(5)]
                    W = T + 4
                    step(V.tensor_scalar(co[b][:, 0:W], xp[b][:, 0:W], w[0], None, ALU.mult))
                    for k in range(1, 5):
                        ins = V.scalar_tensor_tensor(co[b][:, 0:W], xp[b][:, k:k + W], w[k], co[b][:, 0:W],
                                                     ALU.mult, ALU.add)
                        if k < 4:
                            step(ins)
                    ins.then_inc(sem("conv_done"), 1)
            step.restart()
            if STOP <= 1:
                return
            dve.wait_ge(sem("beta_ready"), 1)
            ab = aux[:, 2, 0:192].rearrange("p (c k n) -> p c k n", c=NCH, k=2)
            x3 = gtmp[:, 0:96].rearrange("p (c n) -> p c n", n=16)
            step(V.tensor_tensor(x3, ab[:, :, 1, :], dt_bias.unsqueeze(1).to_broadcast([128, NCH, 16]), ALU.add))
            V.scalar_tensor_tensor(gtmp[:, 96:192], gtmp[:, 0:96], -1.0, gtmp[:, 0:96], ALU.mult, ALU.max)\
                .then_inc(sem("gate_abs"), 1)
            dve.wait_ge(sem("gate_ln"), 1)
            step(V.scalar_tensor_tensor(gtmp[:, 0:96], gtmp[:, 0:96], 0.0, gtmp[:, 96:192], ALU.max, ALU.add))
            V.scalar_tensor_tensor(g_, x3, -1.0, a_log.unsqueeze(1).to_broadcast([128, NCH, 16]), ALU.mult, ALU.mult)\
                .then_inc(sem("gate_ready"), 1)
            dve.wait_ge(sem("gate_tot"), 1)
            step(V.tensor_scalar(negG.rearrange("p c n -> p (c n)"), aux[:, 3, 0:96], -1.0, None, ALU.mult))
            V.tensor_tensor(kdf.rearrange("p c n -> p (c n)"), aux[:, 3, 128:224], negG.rearrange("p c n -> p (c n)"),
                            ALU.add).then_inc(sem("gate_diff"), 1)
            dve.wait_ge(sem("gates_exp"), 1)
            V.tensor_scalar(negE, negE, -1.0, None, ALU.mult).then_inc(sem("gates_done"), 1)
            head_norm(0, 8, lambda n, b: qkvT[:, ds(n + 8 * b, 1), :].rearrange("p o n -> p (o n)"), ALL,
                      lambda b: 128 ** -0.5 if b == 0 else 1.0)
            if STOP <= 2:
                return

            P = [[lin[:, 2 * d + k, :].rearrange("p (h n) -> p h n", n=128) for k in range(2)] for d in range(2)]
            TT = V.tensor_tensor
            dve.wait_ge(sem("state_zero"), 4)
            dve.wait_ge(sem("o_zero"), 1)
            for d in range(2):
                dve.sem_inc(sem(f"state_ready{d}"), 1)

            def delta(n, chunk):
                step.restart()
                for hg in range(2):
                    use = [[0, 0], [0, 0]]

                    def full(d, k):
                        use[d][k] += 1
                        dve.wait_ge(sem(f"bank_full{d}{k}"), n * (2 * USES[k]) + hg * USES[k] + use[d][k])
                        return P[d][k]

                    def read(d, k, ins):
                        ins.then_inc(sem(f"bank_read{d}{k}"), 1)

                    def gate(x, d):
                        return cols(x[:, ds(chunk[d], 1), 8 * d + 4 * hg:8 * d + 4 * hg + 4]
                                    .rearrange("p o n -> p (o n)"))

                    for d in range(2):
                        step(TT(Em[d], full(d, 0), gate(negG, d), ALU.add))
                        V.tensor_scalar(Em[d], Em[d], 0.0, None, ALU.min).then_inc(sem(f"diff_done{d}"), 1)
                    for d in range(2):
                        use[d][0] += 1
                        dve.wait_ge(sem(f"pair_decay{d}"), n * 2 + hg + 1)
                        step(TT(Em[d], Em[d], heads4(C(f"until{d}")), ALU.mult))
                        step(TT(eb[d], Em[d], gate(beta, d), ALU.mult))
                        step(TT(AT[d], full(d, 1), eb[d], ALU.mult))
                        dve.sem_inc(sem(f"bank_read{d}1"), 1)
                        step(TT(Um[d], AT[d], heads4(C(f"level{1 - d}_0")), ALU.mult))
                        step(TT(Um[d], heads4(C("ident")), Um[d], ALU.subtract))
                    for d in range(2):
                        read(d, 1, TT(Em[d], full(d, 1), Em[d], ALU.mult))
                    for d in range(2):
                        step(TT(Tm[d], full(d, 0), heads4(C(f"level{d}_0")), ALU.mult))
                        dve.sem_inc(sem(f"bank_read{d}0"), 1)
                        TT(Tm[d], heads4(C("ident")), Tm[d], ALU.subtract).then_inc(sem(f"inverse{d}"), 1)
                    for lv in range(1, 7):
                        for d in range(2):
                            read(d, 0, TT(gby[d], full(d, 0), heads4(C(f"level{d}_{lv}")), ALU.mult))
                        for d in range(2):
                            if lv < 6:
                                x = full(d, 1)
                                read(d, 1, TT(Tm[d], Tm[d], x, ALU.subtract))
                            x = full(d, 0)
                            step(TT(Um[d], Um[d], x, ALU.subtract))
                            dve.sem_inc(sem(f"bank_read{d}0"), 1)
                            dve.sem_inc(sem(f"inverse{d}"), 1)
                    for d in range(2):
                        step(TT(eb[d], full(d, 1), gate(negE, d), ALU.mult))
                        read(d, 1, TT(eb[d], eb[d], vt[d], ALU.add))
                    for d in range(2):
                        read(d, 0, TT(kts[d], full(d, 0), gate(kdf, d), ALU.mult))
                    for d in range(2):
                        read(d, 1, TT(dl[d], full(d, 1), gate(beta, d), ALU.mult))
                        st = state[2 * hg + d]
                        step(TT(vts[d], st, gate(dec, d), ALU.mult))
                    for d in range(2):
                        o = aT[:, 4 * hg:4 * hg + 4, ds(chunk[d] * 128, 128)]
                        x = full(d, 0)
                        read(d, 0, TT(o, x, o, ALU.add))
                        x = full(d, 1)
                        step(TT(state[2 * hg + d], x, vts[d], ALU.add))
                        dve.sem_inc(sem(f"bank_read{d}1"), 1)
                        dve.sem_inc(sem(f"state_ready{d}"), 1)
                    assert [use[d][k] for d in range(2) for k in range(2)] == [USES[0], USES[1]] * 2, use

            if not SKIP_DELTA:
                with dve.Fori(0, 2) as n:
                    delta(n, [n, dve.snap(n * (-1) + 1)])
                with dve.Fori(2, NCH) as n:
                    delta(n, [n, dve.snap(n * (-1) + 7)])
            step.restart()
            dve.sem_inc(sem("delta_done"), 1)
            if STOP <= 3:
                return
            head_norm(16, 4, lambda n, b: aT[:, ds(n * 2 + b, 1), :].rearrange("p o n -> p (o n)"), ALL,
                      lambda b: dn_g, lambda n, b: zT[:, ds(n * 2 + b, 1), :].rearrange("p o n -> p (o n)"))

            def residual(o, segs, gate_at):
                for i in range(8):
                    dve.wait_ge(tile_done, 8 * o + i + 1)
                    for k, (a, w) in enumerate(segs):
                        c = 0 if a == CTX else 1
                        ins = V.scalar_tensor_tensor(hT[:, i, a:a + w], lin[:, 2 * (i % 2) + k, 0:w],
                                                     mod[:, gate_at + i, c:c + 1], hT[:, i, a:a + w], ALU.mult, ALU.add)
                        if k < len(segs) - 1:
                            ins
                    step(ins)
                    dve.sem_inc(lin_free, 1)
                dve.sem_inc(sem("h_done"), 1)

            dve.wait_ge(sem("x_ready"), 32)
            residual(O_DNOUT, ALL, 16)
            if STOP <= 4:
                return

            def peer(L, segs):
                o_wq, o_uv, nt, u0 = (O_WQ0, O_UV0, NCH, 0) if L == 0 else (O_WQ1, O_UV1, LAT // 128, NCH)
                t0 = segs[0][0]
                with dve.Fori(0, nt) as n:
                    step.restart()
                    dve.wait_ge(sem("tk_kept"), n + (u0 + 1))
                    V.memset(gsum[:, 8:9], 0.0)
                    for m in range(16):
                        step.mark(V.max(tv[:, m, 0:8], sc[:, m, :]))
                    step.wait()
                    for m in range(16):
                        step.mark(V.max_index(ti[:, m, 0:8], tv[:, m, 0:8], sc[:, m, :]))
                        step.mark(V.match_replace(sc2[:, m, :], tv[:, m, 0:8], sc[:, m, :], -3.0e38))
                    step.wait()
                    for m in range(16):
                        step.mark(V.max(tv[:, m, 8:16], sc2[:, m, :]))
                    step.wait()
                    for m in range(16):
                        step.mark(V.max_index(ti[:, m, 8:16], tv[:, m, 8:16], sc2[:, m, :]))
                    step.wait()
                    step.mark(V.tensor_copy(tf, ti))
                    halves = tv.rearrange("p (h s) n -> p h s n", s=2)
                    for h in range(HEADS):
                        step.mark(TT(cand[:, h, :].rearrange("p (a b) -> p a b", a=16),
                                     halves[:, h, 0, :].unsqueeze(2).to_broadcast([128, 16, 16]),
                                     halves[:, h, 1, :].unsqueeze(1).to_broadcast([128, 16, 16]), ALU.add))
                    step.wait()
                    for h in range(HEADS):
                        step.mark(V.max(best[:, h, 0:8], cand[:, h, :]))
                    step.wait()
                    for h in range(HEADS):
                        step.mark(V.max_index(bpos[:, h, 0:8], best[:, h, 0:8], cand[:, h, :]))
                        step.mark(V.match_replace(cand2[:, h, :], best[:, h, 0:8], cand[:, h, :], -3.0e38))
                    step.wait()
                    for h in range(HEADS):
                        step.mark(V.max(best[:, h, 8:16], cand2[:, h, :]))
                    step.wait()
                    for h in range(HEADS):
                        step.mark(V.max_index(bpos[:, h, 8:16], best[:, h, 8:16], cand2[:, h, :]))
                    gate3 = chosen[2].rearrange("p (h n) -> p h n", n=16)
                    TT(gate3, best, best[:, :, 0:1].to_broadcast([128, 8, 16]), ALU.subtract).then_inc(sem("tk_shifted"), 1)
                    step.wait()
                    flat = bpos.rearrange("p h n -> p (h n)")
                    step.mark(V.tensor_scalar(posi[0], flat, 4, None, ALU.logical_shift_right))
                    step.mark(V.tensor_scalar(posi[1], flat, 15, None, ALU.bitwise_and))
                    step.wait()
                    for k in range(2):
                        step.mark(V.tensor_copy(posf[k], posi[k]))
                    step.wait()
                    eq3 = eq.rearrange("p (m a) -> p m a", a=16)
                    for k in range(2):
                        step(TT(eq3, cols(posf[k], 16), C("iota")[:, 0:16].unsqueeze(1).to_broadcast([128, 128, 16]),
                                ALU.is_equal))
                        pick = tf.rearrange("p (h s) a -> p h s a", s=2)[:, :, k, :]
                        step(TT(eq.rearrange("p (h m a) -> p h m a", h=8, a=16), eq.rearrange("p (h m a) -> p h m a", h=8, a=16),
                                pick.unsqueeze(2).to_broadcast([128, 8, 16, 16]), ALU.mult))
                        step(V.reduce_sum(chosen[k], eq3, AX.X))
                    dve.wait_ge(sem("tk_exp"), n + (u0 + 1))
                    step(V.reduce_sum(gsum[:, 0:8], gate3, AX.X))
                    step(V.reciprocal(gsum[:, 0:8], gsum[:, 0:8]))
                    TT(gate3, gate3, cols(gsum[:, 0:8], 16), ALU.mult).then_inc(sem("tk_chosen"), 1)
                step.restart()
                if STOP <= 5:
                    return
                q0 = 32 * u0
                dve.wait_ge(sem("idx_ready"), L + 1)
                with dve.Fori(0, 2 * nt) as n:
                    step.restart()
                    for b in range(2):
                        step(V.tensor_copy(bidx[b], idx[:, :, ds(n * 64 + 32 * b, 32)]))
                        for q in range(8):
                            dve.wait_ge(sem("gb_sum"), n * 16 + (q0 + 8 * b + q + 1))
                            for t in range(4):
                                k, c = 4 * (q % 4) + t, 4 * q + t
                                V.tensor_scalar(hot[0][:, k, :], C("iota"), bidx[b][:, 0, c:c + 1], None, ALU.is_equal)
                                last = V.tensor_scalar(hot[1][:, k, :], C("iota"), bidx[b][:, 1, c:c + 1],
                                                       bidx[b][:, 2, c:c + 1], ALU.is_equal, ALU.mult)
                            last.then_inc(sem("gb_hot"), 1)
                step.restart()
                if STOP <= 6:
                    return

                def multiply(o, g, b, use):
                    dve.wait_ge(sem(f"gg_ready{b}"), use * 16 + (16 + 128 * L))
                    for i in range(8):
                        dve.wait_ge(lin_free, o * 8 + (i + 3 - 8 * O_DN))
                        TT(prod[b][:, i, t0:T], gl[i % 2][:, t0:T], ggate[b][:, t0:T, i], ALU.mult)\
                            .then_inc(sem("p_done"), 1)

                def gather(o):
                    for i in range(8):
                        dve.wait_ge(tile_done, o * 8 + (i + 1))
                        for k, (a, w) in enumerate(segs):
                            last = TT(acc[:, i, a:a + w], lin[:, 2 * (i % 2) + k, 0:w], acc[:, i, a:a + w], ALU.add)
                        last.then_inc(lin_free, 1)

                dve.wait_ge(sem("acc_zero"), L + 1)
                multiply(o_uv, 0, 0, 0)
                with dve.Fori(0, 7) as n:
                    o = n * 4 + o_uv
                    multiply(o + 1, n * 2 + 1, 1, n)
                    gather(o + 2)
                    multiply(o + 3, n * 2 + 2, 0, n + 1)
                    gather(o + 4)
                multiply(o_uv + 29, 15, 1, 7)
                gather(o_uv + 30)
                gather(o_uv + 31)
                dve.wait_ge(lin_free, 8 * (o_uv + 32 - O_DN) + 2)
                for i in range(8):
                    for k, (a, w) in enumerate(segs):
                        c = 0 if a == CTX else 1
                        step.mark(V.scalar_tensor_tensor(hT[:, i, a:a + w], acc[:, i, a:a + w],
                                                         mod[:, 48 * L + 40 + i, c:c + 1], hT[:, i, a:a + w],
                                                         ALU.mult, ALU.add))
                step.wait()
                dve.sem_inc(sem("h_done"), 1)

            norm(1, ALL)
            peer(0, ALL)
            if STOP <= 7:
                return
            norm(2, ALL)
            dve.wait_ge(sem("lambdas_ready"), 16)
            step(TT(lamv[:, :, 0, :], lamv[:, :, 0, :], lamv[:, :, 1, :], ALU.mult))
            V.reduce_sum(lam[:, 0:2], lamv[:, :, 0, :], AX.X).then_inc(sem("lam_sums"), 1)
            dve.wait_ge(sem("lam_exp"), 1)
            step(TT(lam[:, 2:3], lam[:, 0:1], lam[:, 1:2], ALU.subtract))
            step(V.tensor_scalar(lam[:, 2:3], lam[:, 2:3], LAMBDA_INIT, None, ALU.add))
            step(V.tensor_scalar(da_qg, da_qg, 64 ** -0.5, None, ALU.mult))
            step(V.tensor_scalar(da_sg, da_sg, 1.0 - LAMBDA_INIT, None, ALU.mult))
            one = lambda x, n, b: x[:, ds(n * 2 + b, 1), :].rearrange("p o n -> p (o n)")
            head_norm(24, 4, lambda n, b: one(qT, n, b), ONLY_LAT, lambda b: da_qg, rt=rta)
            head_norm(32, 4, lambda n, b: one(kT, n, b), ALL, lambda b: da_kg, rt=rta)
            dve.wait_ge(sem("hn_out"), 42)
            dve.wait_ge(sem("rope_ready"), 16)
            with dve.Fori(0, 8) as n:
                step.restart()
                for b in range(2):
                    x = (kT if b else qT)[:, ds(n, 1), CTX:T].rearrange("p o n -> p (o n)")
                    step.mark(TT(rtmp[b][0], x, rope[:, 0, :], ALU.mult))
                    dve.wait_ge(sem("rope_turned"), n * 2 + (b + 1))
                    step(TT(rtmp[b][1], aux[:, b, :], rope[:, 1, :], ALU.mult))
                    TT(x, rtmp[b][0], rtmp[b][1], ALU.add).then_inc(sem("rope_done"), 1)
            step.restart()
            with dve.Fori(0, LAT // 128) as n:
                step.restart()

                def maxima(h):
                    dve.wait_ge(sem("at_scores"), n * 8 + (h + 1))
                    m = mx[:, 4 * (h % 2):4 * (h % 2) + 4]
                    for c in range(2):
                        step.mark(V.tensor_reduce(m[:, c:c + 1], aux[:, 2 * c:2 * c + 2, 0:T // 2], AX.XY, ALU.max))
                    step.wait()
                    V.tensor_scalar(m[:, 2:4], m[:, 0:2], -1.0, None, ALU.mult).then_inc(sem("at_max"), 1)
                maxima(0)
                for h in range(8):
                    dve.wait_ge(sem("at_exp"), n * 8 + (h + 2))
                    z = mx[:, 8 + 4 * (h % 2):12 + 4 * (h % 2)]
                    step(V.reciprocal(z[:, 2:4], z[:, 0:2]))
                    step(TT(z[:, 3:4], z[:, 3:4], lam[:, 2:3], ALU.mult))
                    step(V.tensor_scalar(pr[h % 2][1], pr[h % 2][1], z[:, 3:4], None, ALU.mult))
                    V.scalar_tensor_tensor(pr[h % 2][0], pr[h % 2][0], z[:, 2:3], pr[h % 2][1], ALU.mult, ALU.subtract)\
                        .then_inc(sem("at_weights"), 1)
                    if h < 7:
                        maxima(h + 1)
                    dve.wait_ge(sem("at_out"), n * 8 + (h + 1))
                    V.tensor_copy(aT[:, h, ds(n * 128 + CTX, 128)], lin[:, 2, 0:128]).then_inc(sem("at_kept"), 1)
                dve.sem_inc(sem("at_used"), 1)
            step.restart()
            dve.wait_ge(sem("at_kept"), 33)
            head_norm(40, 4, lambda n, b: one(aT, n, b), ONLY_LAT, lambda b: da_sg, rt=rta)
            residual(O_DAOUT, ONLY_LAT, 64)
            if STOP <= 8:
                return
            norm(3, ONLY_LAT)
            peer(1, ONLY_LAT)


USES = [17, 10]
H_END = 4
LAST_OCTET = O_END


def DB(k):
    return 1


def kernel(**inputs):
    from concourse import bacc
    from concourse.bass_utils import run_bass_kernel_spmd

    f = {k: np.asarray(v) for k, v in inputs.items()}

    def tiles(w):
        return w.reshape(KC, 128, -1, 128).transpose(2, 1, 0, 3)

    def experts(u, v):
        u = u.reshape(128, NG, 8, KC, 128).transpose(1, 2, 4, 3, 0)
        v = v.reshape(128, NG, 8, 8, 128).transpose(1, 3, 0, 2, 4)
        order = [u[0]]
        for g in range(1, NG):
            order += [u[g], v[g - 1]]
        return order + [v[NG - 1]]

    def feature(v):
        return np.moveaxis(v.reshape(v.shape[:-1] + (KC, 128)), -1, 0)

    parts = [tiles(f["ada_w"][0]), tiles(f["ada_w"][1]), tiles(f["dn_w_in"][0][:, :4 * D]), tiles(f["dn_w_out"][0]),
             tiles(f["peer_wq"][0]), *experts(f["peer_u"][0], f["peer_v"][0]),
             tiles(f["da_w_qkv"][0]), tiles(f["da_w_out"][0]), tiles(f["peer_wq"][1]),
             *experts(f["peer_u"][1], f["peer_v"][1])]
    weights = np.concatenate(parts, 0)
    assert weights.shape[0] == 8 * O_END
    tokens = np.concatenate([f["ctx"][0], f["x"][0]], 0)
    rows = lambda v: np.broadcast_to(v.reshape(1, -1), (128, v.size))
    norms = np.stack([f["norm1_g"][0], f["norm2_g"][0], f["norm1_g"][1], f["norm2_g"][1]])
    params = np.concatenate([
        feature(np.stack([f["c"][0], f["c_ctx"]])).transpose(0, 2, 1).reshape(128, 16),
        f["ada_b"].reshape(96, 128).T,
        feature(norms).reshape(128, 32),
        f["dn_norm_g"][0][:, None], np.tile(f["da_q_norm_g"][0], 2)[:, None], np.tile(f["da_k_norm_g"][0], 2)[:, None],
        f["da_subln_g"][0][:, None],
        f["dn_conv"][0].reshape(5, 24, 128).transpose(2, 1, 0).reshape(128, 120),
        rows(f["dn_dt_bias"]), rows(f["dn_a_log"])], 1)
    where, const = const_table()
    arrays = {
        "weights": weights, "params": params, "const": const, "rope": rope_table(),
        "x": tokens.T.reshape(KC, 128, T).transpose(1, 0, 2),
        "w_ab": f["dn_w_in"][0][:, 4 * D:].reshape(KC, 128, 32).transpose(1, 0, 2),
        "lambdas": np.broadcast_to(f["da_lambda"][0].reshape(1, 256), (128, 256)),
        "keys": f["peer_keys"].reshape(2, 16, 128, 128).transpose(0, 3, 1, 2),
    }
    arrays = {k: np.ascontiguousarray(v) for k, v in arrays.items()}
    nc = bacc.Bacc("TRN2", target_bir_lowering=False, num_devices=1, dynamic_dma_scratch_size=1024)
    io = {k: nc.dram_tensor(f"in_{k}", v.shape, F32, kind="ExternalInput").ap() for k, v in arrays.items()}
    io["out"] = nc.dram_tensor("out_0", (128, KC, LAT), F32, kind="ExternalOutput").ap()
    backbone(nc, io, where)
    r = run_bass_kernel_spmd(nc, [{f"in_{k}": v for k, v in arrays.items()}], core_ids=[0])
    out = np.asarray(r.results[0]["out_0"])
    return np.ascontiguousarray(out.transpose(2, 1, 0).reshape(1, LAT, D))
```

```python
from contextlib import ExitStack
import math

import numpy as np
import concourse.bass as bass
from concourse import mybir

F32 = mybir.dt.float32
F32R = mybir.dt.float32r
U32 = mybir.dt.uint32
ALU = mybir.AluOpType
ACT = mybir.ActivationFunctionType
AX = mybir.AxisListType
ds = bass.ds

D = 1024
KC = D // 128
CTX, LAT = 256, 512
T = CTX + LAT
HEADS = 8
EPS = 1e-6
NCH = T // 128
NG = 16
LAMBDA_INIT = 0.8 - 0.6 * math.exp(-0.3)
ALL = [(0, CTX), (CTX, LAT)]
ONLY_LAT = [(CTX, LAT)]

O_ADA, O_DN, O_DNOUT, O_WQ0, O_U0, O_V0, O_QKV, O_DAOUT, O_WQ1, O_U1, O_V1, O_END = (
    0, 12, 16, 17, 19, 35, 51, 54, 55, 57, 73, 89)
ADA = 8 * O_DN
USES = [17, 10]
LIN0 = -8 * O_DN
LINV0 = 8 * O_V0 + LIN0 - 16 * O_V0
LIN1 = 16 * O_QKV + LINV0 - 8 * O_QKV
LINV1 = 8 * O_V1 + LIN1 - 16 * O_V1


def const_table():
    i, j = np.arange(128)[:, None], np.arange(128)[None, :]
    parts = {"ident": i == j, "ones": np.ones((128, 128)), "mean1024": np.full((128, 128), 1 / 1024),
             "mean128": np.full((128, 128), 1 / 128), "mean64": (i // 64 == j // 64) / 64.0,
             "until0": i <= j, "until1": i >= j}
    for n in range(7):
        b = 1 << n
        m = (i // (2 * b) == j // (2 * b)) & ((i // b) % 2 == 1) & ((j // b) % 2 == 0)
        parts[f"level0_{n}"], parts[f"level1_{n}"] = m, m.T
    same = i // 64 == j // 64
    parts["rotate"] = (np.where(same & (i % 64 == j % 64 + 32), -1.0, 0)
                       + np.where(same & (i % 64 == j % 64 - 32), 1.0, 0))
    parts["iota"] = np.broadcast_to(np.arange(128), (128, 128))
    where, at, cols = {}, 0, []
    for name, a in parts.items():
        where[name] = at
        at += a.shape[1]
        cols.append(np.asarray(a, np.float32))
    return where, np.ascontiguousarray(np.concatenate(cols, 1))


def rope_table():
    inv = (np.float32(10000.0) ** (-np.arange(16, dtype=np.float32) / np.float32(16))).astype(np.float32)
    tok = np.arange(LAT)
    row, col = (tok // 64).astype(np.float32), (tok % 64).astype(np.float32)
    ang = np.concatenate([row[:, None] * inv, col[:, None] * inv], 1).astype(np.float32)
    return np.ascontiguousarray(np.stack([np.tile(np.cos(ang).T, (4, 1)), np.tile(np.sin(ang).T, (4, 1))], 1))


def backbone(nc, io, where):
    with ExitStack() as ctx:
        sems = {}

        def sem(name):
            if name not in sems:
                sems[name] = ctx.enter_context(nc.semaphore(name))
            return sems[name]

        NCONST = max(where.values()) + 128
        spot = [1152]

        def here():
            return spot[0]

        def at(name, shape, dt=F32, place=None):
            words = int(np.prod(shape[1:]))
            if place is None:
                place = spot[0]
                spot[0] += 4 * words
            return nc.alloc_sbuf_tensor_at(name, shape, dt, offset=place)

        const = at("const", [128, NCONST])

        def C(name):
            return const[:, where[name]:where[name] + 128]

        raw = at("raw", [128, 4, KC, 128])
        wH = at("weight_high", [128, 2, KC, 128], F32R)
        wL = at("weight_low", [128, 2, KC, 128], F32R)
        hT = at("hT", [128, KC, T])
        oT = at("oT", [128, KC, T], place=here())
        ada_rows = at("ada_rows", [128, 12 * D], place=here())
        aH = at("act_high", [128, KC, T], F32R)
        low = at("low_scratch", [128, KC * T], place=here())
        aL = at("act_low", [128, KC, T], F32R)
        mod = at("mod", [128, 96, 2])
        gates = at("gates", [128, 6, NCH, 16])
        small = at("small", [128, 512])
        PROD0 = 16 * T
        arena0 = here()
        prodH = at("prod_high", [128, 2, 4, T], F32R, place=arena0 + 4 * PROD0)
        prodL = at("prod_low", [128, 2, 4, T], F32R, place=arena0 + 4 * (PROD0 + 8 * T))
        ARENA = 34 * T + 8
        arena = at("arena", [128, ARENA])
        assert here() <= 229368
        lin = ctx.enter_context(nc.psum_tensor("lin", [128, 4, 512], F32))
        aux = ctx.enter_context(nc.psum_tensor("aux", [128, 4, 512], F32))

        taken = [0]

        def sm(w):
            taken[0] += w
            assert taken[0] <= 512
            return small[:, taken[0] - w:taken[0]]

        params = sm(16 + 96 + 32 + 4 + 120 + 32)
        cond = params[:, 0:16].rearrange("p (k c) -> p k c", c=2)
        ada_b = params[:, 16:112]
        norm_g = params[:, 112:144]
        dn_g, da_qg, da_kg, da_sg = (params[:, 144 + n:145 + n] for n in range(4))
        conv_w = params[:, 148:268]
        dt_bias = params[:, 268:284]
        a_log = params[:, 284:300]
        gsc = sm(64).rearrange("p (q k c) -> p q k c", q=4, c=2)
        eps = sm(1)
        lam = sm(8)
        mx = sm(32)

        def Rg(a, w):
            assert a + w <= ARENA
            return arena[:, a:a + w]

        qkvT = Rg(0, 24 * T).rearrange("p (t n) -> p t n", n=T)
        zT = Rg(24 * T, 8 * T).rearrange("p (t n) -> p t n", n=T)
        nT = Rg(0, 8 * T).rearrange("p (k n) -> p k n", n=T)
        SCR = 32 * T
        XPW = T + 8
        ada_w = [Rg(8192 * b, 8192).rearrange("p (t k n) -> p t k n", t=8, k=KC) for b in range(3)]
        ada_sum = [x[0:2, 2 * b:2 * b + 2, :] for x, b in ((aux, 0), (aux, 1), (lin, 0))]
        wab = Rg(SCR, 32 * KC).rearrange("p (k n) -> p k n", k=KC)
        gtmp = Rg(SCR + 32 * KC, 4 * 96)
        nrt = Rg(SCR + 32 * KC + 4 * 96, T)
        hflat = hT[:, :, :].rearrange("p k n -> p (k n)")
        xp = [hflat[:, b * XPW:(b + 1) * XPW] for b in range(2)]
        co = [hflat[:, (2 + b) * XPW:(3 + b) * XPW] for b in range(2)]
        sq = [hflat[:, 4 * XPW + b * T:4 * XPW + (b + 1) * T] for b in range(2)]
        rt = [xp[b][:, 0:T] for b in range(2)]
        sq2 = [Rg(b * T, T) for b in range(2)]
        rt2 = [Rg((2 + b) * T, T) for b in range(2)]
        beta, g_, negG, negE, kdf, dec = (gates[:, n, :, :] for n in range(6))

        blocks = [Rg(SCR + 512 * n, 512) for n in range(2)] + \
                 [x[:, 512 * n:512 * n + 512] for x in (low, hflat) for n in range(KC * T // 512)]

        def four(x):
            return x.rearrange("p (h n) -> p h n", n=128)

        blk = [four(x) for x in blocks]
        (kts, vts, gby, vt, egq, Em, eb, AT, Tm, Um, dl) = ([blk[2 * n + d] for d in range(2)] for n in range(11))
        state = [blk[22 + n] for n in range(4)]

        pqT = Rg(0, 16 * T).rearrange("p (m n) -> p m n", n=T)
        K0 = 16 * T
        keys = Rg(K0, 2048).rearrange("p (m n) -> p m n", n=128)
        X0, Y0, S0 = K0 + 2048, K0 + 4096, K0 + 6144
        qs = Rg(X0, 2048).rearrange("p (m n) -> p m n", n=128)
        sc2 = Rg(X0, 2048).rearrange("p (m n) -> p m n", n=128)
        cand = Rg(X0, 2048).rearrange("p (m n) -> p m n", n=256)
        sc = Rg(Y0, 2048).rearrange("p (m n) -> p m n", n=128)
        cand2 = Rg(Y0, 2048).rearrange("p (m n) -> p m n", n=256)
        eq = Rg(Y0, 2048)
        sp_ = [Rg(S0 + 128 * n, 128) for n in range(16)]
        tv = Rg(S0, 256).rearrange("p (m n) -> p m n", n=16)
        ti = Rg(S0 + 256, 256).bitcast(U32).rearrange("p (m n) -> p m n", n=16)
        tf = Rg(S0 + 512, 256).rearrange("p (m n) -> p m n", n=16)
        best = sp_[6].rearrange("p (m n) -> p m n", n=16)
        bpos = sp_[7].bitcast(U32).rearrange("p (m n) -> p m n", n=16)
        posi = [sp_[8].bitcast(U32), sp_[9].bitcast(U32)]
        posf = [sp_[10], sp_[11]]
        chosen = [sp_[12], sp_[13], sp_[14]]
        gsum = sp_[15]
        idx = Rg(S0 + 2048, 3 * T).rearrange("p (k n) -> p k n", n=T)
        gl = [Rg(S0 + 2048 + (3 + b) * T, T) for b in range(2)]
        TB = 16
        stage = [Rg(b * 128 * TB, 128 * TB) for b in range(2)]
        GB = 2 * 128 * TB
        hot = [at(f"hot{n}", [128, 16, 128], F32R, place=arena0 + 4 * (GB + 2048 * n)) for n in range(3)]
        bidx = Rg(GB + 3 * 2048, 4 * 96).rearrange("p (k n) -> p k n", k=4)
        bhigh = at("gate_high", [128, 96], F32R, place=arena0 + 4 * (GB + 3 * 2048 + 4 * 96))
        gate_dram = nc.dram_tensor("gate_matrix", (NG, 128, T * 8), F32).ap()
        gelu_dram = nc.dram_tensor("gelu", (128, 128, T), F32).ap()
        ggate = [Rg(8 * b * T, 8 * T).rearrange("p (n c) -> p n c", c=8) for b in range(2)]
        hb = [Rg((32 + b) * T, T) for b in range(2)]
        qT = Rg(0, 8 * T).rearrange("p (c n) -> p c n", n=T)
        kT = Rg(8 * T, 8 * T).rearrange("p (c n) -> p c n", n=T)
        vtok = Rg(16 * T, 8 * T).rearrange("p (c n) -> p c n", n=D)
        A0 = 24 * T
        qst = Rg(A0, D).rearrange("p (c n) -> p c n", n=128)
        pr = [[Rg(A0 + D + (2 * b + c) * T, T) for c in range(2)] for b in range(2)]
        wtt = Rg(A0 + D + 4 * T, T).rearrange("p (c n) -> p c n", n=128)
        at_scores = [x[:, 0:3, :].rearrange("p b n -> p (b n)") for x in (aux, lin)]
        at_turn = [aux[:, 3, :], lin[:, 3, :]]
        lamv = Rg(A0 + D + 5 * T, 256).rearrange("p (a b n) -> p a b n", a=2, b=2)
        rope = Rg(A0 + D + 5 * T + 256, 2 * LAT).rearrange("p (a n) -> p a n", a=2)
        rtmp = [[Rg(A0 + D + (2 * b + c) * T, LAT) for c in range(2)] for b in range(2)]
        assert A0 + D + 5 * T + 256 + 2 * LAT <= ARENA
        sqa, rta = [pr[0][0], pr[0][1]], [pr[1][0], pr[1][1]]

        w_ready = [sem(f"weight_ready{i}") for i in range(8)]
        tile_done, lin_free = sem("tile_done"), sem("lin_free")
        raw_used, w_high, v_half = sem("raw_used"), sem("weight_high"), sem("v_half")

        def peer_shape(L):
            if L == 0:
                return O_WQ0, O_U0, O_V0, NCH, 0, LIN0
            return O_WQ1, O_U1, O_V1, LAT // 128, NCH, LIN1

        class Steps:

            def __init__(self, eng, name):
                self.eng, self.sem, self.n = eng, sem(name), 0

            def mark(self, ins):
                ins.then_inc(self.sem, 1)
                self.n += 1

            def wait(self):
                self.eng.wait_ge(self.sem, self.n)

            def __call__(self, ins):
                self.mark(ins)
                self.wait()

            def restart(self):
                self.eng.sem_clear(self.sem)
                self.n = 0

        def heads4(x):
            return x.unsqueeze(1).to_broadcast([128, 4, 128])

        def cols(x, n=128):
            return x.unsqueeze(2).to_broadcast([128, x.shape[1], n])

        def half(x, lv, odd):
            if len(x.shape) == 3:
                return x.rearrange("p h (m two b) -> p (h m) two b", two=2, b=1 << lv)[:, :, odd, :]
            return x.rearrange("p (m two b) -> p m two b", two=2, b=1 << lv)[:, :, odd, :]

        def ada_loads(eng, first):
            for o in range(first, O_DN, 2):
                if o >= 3:
                    eng.wait_ge(sem("ada_used"), o - 2)
                eng.dma_start(ada_w[o % 3].rearrange("p t k n -> p t (k n)"),
                              io["weights"][8 * o:8 * o + 8].rearrange("t p k n -> p t (k n)"))\
                    .then_inc(sem(f"ada_ready{o % 3}"), 16)

        block = ctx.enter_context(nc.Block())

        @block.sync
        def _(sp):
            sp.dma_start(params, io["params"]).then_inc(sem("params_ready"), 16)
            sp.dma_start(const[:, :], io["const"]).then_inc(sem("const_ready"), 16)
            ada_loads(sp, 0)
            sp.dma_start(hT[:, :, :], io["x"]).then_inc(sem("x_ready"), 16)
            sp.dma_start(wab, io["w_ab"]).then_inc(sem("wab_ready"), 16)
            for i in range(8):
                if i >= 4:
                    sp.wait_ge(raw_used, i - 3)
                sp.dma_start(raw[:, i % 4, :, :], io["weights"][ADA + i]).then_inc(w_ready[i], 16)
            with sp.Fori(O_DN + 1, O_END) as o:
                for i in range(8):
                    sp.wait_ge(raw_used, o * 8 + (i - 3 - ADA))
                    sp.dma_start(raw[:, i % 4, :, :], io["weights"][ds(o * 8 + i, 1), :, :, :].rearrange("o p k n -> (o p) k n"))\
                        .then_inc(w_ready[i], 16)
            sp.wait_ge(sem("h_done"), 4)
            sp.dma_start(io["out"], hT[:, :, CTX:T]).then_inc(sem("out_done"), 16)
            sp.wait_ge(sem("out_done"), 16)

        @block.tensor
        def _(pe):
            def octet(o, tile):
                for i in range(8):
                    pe.wait_ge(raw_used, o * 8 + (i + 1 - ADA))
                    tile(i).then_inc(tile_done, 1)

            def parts(out, w, a, start, stop):
                nc.tensor.matmul(out, w(wH), a(aH, prodH), start=start, stop=False)
                nc.tensor.matmul(out, w(wH), a(aL, prodL), start=False, stop=False)
                return nc.tensor.matmul(out, w(wL), a(aH, prodH), start=False, stop=stop)

            def lin_octet(o, off, segs=ALL, more=None):
                def tile(i):
                    pe.wait_ge(lin_free, o * 8 + (i + 1 + off))
                    for k, (a, w) in enumerate(segs):
                        for kc in range(KC):
                            last = parts(lin[:, 2 * (i % 2) + k, 0:w], lambda x: x[:, i % 2, kc, :],
                                         lambda x, _: x[:, kc, a:a + w], kc == 0, kc == KC - 1)
                    return last
                if more is None:
                    return octet(o, tile)
                for i in range(8):
                    pe.wait_ge(raw_used, o * 8 + (i + 1 - ADA))
                    tile(i).then_inc(tile_done, 1)
                    more(i)

            def norm(q, segs):
                for kc in range(KC):
                    pe.wait_ge(sem("norm_sq"), 8 * q + kc + 1)
                    for k, (a, w) in enumerate(segs):
                        last = nc.tensor.matmul(aux[:, k, 0:w], C("mean1024"), nT[:, kc, a:a + w],
                                                start=kc == 0, stop=kc == KC - 1)
                last.then_inc(sem("norm_sum"), 1)

            def peer(L, segs):
                o_wq, o_u, o_v, nt, u0, off = peer_shape(L)
                pe.wait_ge(sem("norm_done"), 16 * (2 * L + 2))
                with pe.Fori(o_wq, o_wq + 2) as o:
                    lin_octet(o, off, segs)
                pe.wait_ge(sem("keys_ready"), 16 * (L + 1))
                with pe.Fori(0, nt) as n:
                    pe.wait_ge(sem("tk_query"), n + (u0 + 1))
                    for m in range(16):
                        last = nc.tensor.matmul(aux[:, m // 4, 128 * (m % 4):128 * (m % 4) + 128], qs[:, m, :],
                                                keys[:, m, :], start=True, stop=True)
                    last.then_inc(sem("tk_scores"), 1)
                    lin_octet(n + o_u, off, segs)
                    pe.wait_ge(sem("tk_chosen"), n + (u0 + 1))
                    for k in range(3):
                        last = nc.tensor.transpose(aux[:, 0, 128 * k:128 * k + 128], chosen[k], C("ident"))
                    last.then_inc(sem("tk_turned"), 1)
                q0 = 32 * u0
                with pe.Fori(0, 8) as n:
                    def quads(i):
                        for q in range(nt * i // 2, nt * (i + 1) // 2):
                            pe.wait_ge(sem("gb_hot"), n * (4 * nt) + (q0 + q + 1))
                            pe.wait_ge(sem("gb_kept"), n * (4 * nt) + (q0 + q + 1))
                            for t in range(4):
                                k = 4 * (q % 4) + t
                                for j in (1, 2):
                                    last = nc.tensor.matmul(aux[:, q % 4, 128 * t:128 * t + 128], hot[0][:, k, :],
                                                            hot[j][:, k, :], start=j == 1, stop=j == 2)
                            last.then_inc(sem("gb_sum"), 1)
                    lin_octet(n + (o_u + nt), off, segs, quads)
                with pe.Fori(o_u + nt + 8, o_v) as o:
                    lin_octet(o, off, segs)
                offv = LINV1 if L else LINV0
                with pe.Fori(o_v, o_v + 16) as o:
                    for i in range(8):
                        pe.wait_ge(raw_used, o * 8 + (i + 1 - ADA))
                        if i % 4 == 0:
                            pe.wait_ge(sem("p_done"), o * 8 + (i + 4 + 128 * L - 8 * o_v))
                        for s in range(2):
                            pe.wait_ge(lin_free, o * 16 + (2 * i + s + 1 + offv))
                            for k, (a, w) in enumerate(segs):
                                for c in range(4):
                                    last = parts(lin[:, 2 * s + k, 0:w], lambda x: x[:, i % 2, 4 * s + c, :],
                                                 lambda _, x: x[:, i // 4, c, a:a + w], c == 0, c == 3)
                            last.then_inc(tile_done if s else v_half, 1)

            def head_norm(base, iters, ones, segs, sq=sq):
                with pe.Fori(0, iters) as n:
                    for b in range(2):
                        pe.wait_ge(sem("hn_sq"), n * 2 + (base + b + 1))
                        pe.wait_ge(sem("hn_root"), n * 2 + (base + b + 1))
                        for k, (a, w) in enumerate(segs):
                            last = nc.tensor.matmul(aux[:, 2 * b + k, 0:w], ones, sq[b][:, a:a + w],
                                                    start=True, stop=True)
                        last.then_inc(sem("hn_sum"), 1)

            pe.wait_ge(sem("cond_ready"), 1)
            with pe.Fori(0, O_DN // 3) as n:
                for b in range(3):
                    pe.wait_ge(sem(f"ada_ready{b}"), n * 16 + 16)
                    pe.wait_ge(sem("ada_row"), n * 3 + (b + 1))
                    for k in range(2):
                        for kc in range(KC):
                            last = nc.tensor.matmul(ada_sum[b][:, k, :], cond[:, kc, :], ada_w[b][:, 4 * k:4 * k + 4, kc, :],
                                                    start=kc == 0, stop=kc == KC - 1)
                    last.then_inc(sem("ada_used"), 1)
            pe.wait_ge(sem("const_ready"), 16)
            pe.wait_ge(sem("ada_row"), 3 + O_DN)
            for i in range(ADA):
                last = nc.tensor.transpose(aux[:, 0, 2 * i:2 * i + 2], ada_rows[0:2, 128 * i:128 * i + 128],
                                           C("ident")[0:2, 0:2])
            last.then_inc(sem("ada_turned"), 1)
            pe.wait_ge(sem("ada_read"), 1)
            pe.wait_ge(sem("const_ready"), 16)
            norm(0, ALL)

            pe.wait_ge(sem("norm_done"), 16)
            pe.wait_ge(sem("wab_ready"), 16)
            for t in range(NCH):
                for kc in range(KC):
                    for k, x in enumerate((aL, aH)):
                        last = nc.tensor.matmul(aux[:, 2, 32 * t:32 * t + 32],
                                                x[:, kc, 128 * t:128 * t + 128].bitcast(F32), wab[:, kc, :],
                                                start=kc + k == 0, stop=kc + k == KC)
            last.then_inc(sem("gate_sum"), 1)
            with pe.Fori(O_DN, O_DN + 4) as o:
                lin_octet(o, LIN0)
            pe.wait_ge(sem("gate_ready"), 1)
            for d in range(2):
                nc.tensor.matmul(aux[:, 3, 0:96].rearrange("p (c n) -> p c n", n=16)[:, :, 8 * d:8 * d + 8],
                                 C(f"until{d}"), g_[:, :, 8 * d:8 * d + 8], start=True, stop=True)
            nc.tensor.matmul(aux[:, 3, 128:224], C("ones"), g_.rearrange("p c n -> p (c n)"),
                             start=True, stop=True).then_inc(sem("gate_tot"), 1)
            pe.wait_ge(sem("gates_done"), 1)
            head_norm(0, 8, C("ones"), ALL)

            P = [[lin[:, 2 * d + k, :].rearrange("p (h n) -> p h n", n=128) for k in range(2)] for d in range(2)]

            def each(out, lhs, rhs, start=True, stop=True, op=None):
                for h in range(4):
                    last = nc.tensor.matmul(out[:, h, :], lhs(h), rhs(h), start=start, stop=stop)
                return last

            def each_half(out, lhs, rhs, lv, odd):
                for h in range(4):
                    last = nc.tensor.matmul(half(out[:, h, :], lv, odd), lhs[:, h, :], half(rhs[:, h, :], lv, odd),
                                            start=True, stop=True)
                return last

            def delta(n, chunk):
                for hg in range(2):
                    use = [[0, 0], [0, 0]]

                    def bank(d, k):
                        pe.wait_ge(sem(f"bank_read{d}{k}"), n * (2 * USES[k]) + hg * USES[k] + use[d][k] + 1)
                        use[d][k] += 1
                        return P[d][k]

                    def full(d, k, last):
                        last.then_inc(sem(f"bank_full{d}{k}"), 1)

                    for d in range(2):
                        pe.wait_ge(sem(f"staged{d}"), n * 4 + 2 * hg + 1)
                        full(d, 0, each(bank(d, 0), lambda h: gby[d][:, h, :], lambda h: C(f"until{d}")))
                    for d in range(2):
                        pe.wait_ge(sem(f"staged{d}"), n * 4 + 2 * hg + 2)
                        full(d, 1, each(bank(d, 1), lambda h: kts[d][:, h, :], lambda h: kts[d][:, h, :]))
                    for d in range(2):
                        out = bank(d, 0)
                        for h in range(4):
                            last = nc.tensor.transpose(out[:, h, :], vts[d][:, h, :], C("ident"))
                        full(d, 0, last)
                    for d in range(2):
                        full(d, 1, each(bank(d, 1), lambda h: kts[d][:, h, :],
                                        lambda h: qkvT[:, 4 * hg + h, ds(chunk[d] * 128, 128)]))
                    for d in range(2):
                        full(d, 0, each(bank(d, 0), lambda h: AT[d][:, h, :], lambda h: C("ident")))
                    for lv in range(1, 7):
                        for d in range(2):
                            if lv == 1:
                                pe.wait_ge(sem(f"inverse{d}"), n * 2 + hg + 1)
                            full(d, 0, each(bank(d, 0), lambda h: AT[d][:, h, :], lambda h: Tm[d][:, h, :]))
                        for d in range(2):
                            out1, out0 = bank(d, 1), bank(d, 0)
                            if lv < 6:
                                full(d, 1, each_half(out1, Um[d], gby[d], lv, d))
                            full(d, 0, each_half(out0, gby[d], Um[d], lv, 1 - d))
                            if lv == 6:
                                use[d][1] -= 1
                    for d in range(2):
                        pe.wait_ge(sem(f"state_ready{d}"), n * 2 + hg + 1)
                        full(d, 1, each(bank(d, 1), lambda h: kts[d][:, h, :], lambda h: state[2 * hg + d][:, h, :]))
                    for d in range(2):
                        out = bank(d, 0)
                        for h in range(4):
                            last = nc.tensor.transpose(out[:, h, :], kts[d][:, h, :], C("ident"))
                        full(d, 0, last)
                    for d in range(2):
                        out = bank(d, 1)
                        full(d, 1, each(out, lambda h: Um[d][:, h, :], lambda h: eb[d][:, h, :]))
                    for d in range(2):
                        pe.wait_ge(sem(f"q_decayed{d}"), n * 2 + hg + 1)
                        out0, out1 = bank(d, 0), bank(d, 1)
                        for h in range(4):
                            nc.tensor.matmul(out0[:, h, :], state[2 * hg + d][:, h, :], egq[d][:, h, :],
                                             start=True, stop=False)
                            last = nc.tensor.matmul(out0[:, h, :], dl[d][:, h, :], Em[d][:, h, :],
                                                    start=False, stop=True)
                        full(d, 0, last)
                        full(d, 1, each(out1, lambda h: kts[d][:, h, :], lambda h: dl[d][:, h, :]))

            with pe.Fori(0, 2) as n:
                delta(n, [n, pe.snap(n * (-1) + 1)])
            with pe.Fori(2, NCH) as n:
                delta(n, [n, pe.snap(n * (-1) + 7)])
            pe.wait_ge(sem("delta_done"), 1)
            head_norm(16, 4, C("mean128"), ALL, sq2)
            pe.wait_ge(sem("hn_out"), 2 + 24)
            lin_octet(O_DNOUT, LIN0)
            norm(1, ALL)
            peer(0, ALL)
            norm(2, ALL)

            pe.wait_ge(sem("norm_done"), 48)
            lin_octet(O_QKV, LIN1, ONLY_LAT)
            lin_octet(O_QKV + 1, LIN1)

            def v_tile(i):
                pe.wait_ge(lin_free, 8 * (O_QKV + 2) + LIN1 + i + 1)
                for t in range(NCH):
                    for kc in range(KC):
                        for k, (x, w) in enumerate(((aH, wH), (aH, wL), (aL, wH))):
                            last = nc.tensor.matmul(lin[:, 2 * (i % 2) + t // 3, (t % 3) * 128:(t % 3) * 128 + 128],
                                                    x[:, kc, 128 * t:128 * t + 128], w[:, i % 2, kc, :],
                                                    start=kc + k == 0, stop=kc + k == KC + 1)
                return last
            octet(O_QKV + 2, v_tile)
            head_norm(24, 4, C("mean64"), ONLY_LAT, sqa)
            head_norm(32, 4, C("mean64"), ALL, sqa)
            pe.wait_ge(sem("hn_out"), 2 + 40)
            with pe.Fori(0, 8) as n:
                for b in range(2):
                    pe.wait_ge(sem("rope_done"), n * 2 + (b + 1))
                    x = (kT if b else qT)[:, ds(n, 1), CTX:T].rearrange("p o n -> p (o n)")
                    nc.tensor.matmul(aux[:, b, :], C("rotate"), x, start=True, stop=True)\
                        .then_inc(sem("rope_turned"), 1)
            pe.wait_ge(sem("rope_done"), 18)
            with pe.Fori(0, LAT // 128) as n:
                pe.wait_ge(sem("at_query"), n + 1)

                def scores(h):
                    pe.wait_ge(sem("at_exp"), n * 8 + (h + 1))
                    for c, k0, k1 in ((0, 512, T), (0, 0, 512), (1, 1024 - T, T), (1, 0, 1024 - T)):
                        if c == 1 and k0 == 0:
                            pe.wait_ge(sem("at_shared"), n * 8 + (h + 1))
                        last = nc.tensor.matmul(at_scores[h % 2][:, T * c + k0:T * c + k1], qst[64 * c:64 * c + 64, h, :],
                                                kT[64 * c:64 * c + 64, h, k0:k1], start=True, stop=True)
                        if k0 == 512:
                            last.then_inc(sem("at_shared"), 1)
                    last.then_inc(sem("at_scores"), 1)
                scores(0)
                scores(1)
                for h in range(8):
                    pe.wait_ge(sem("at_weights"), n * 8 + (h + 1))
                    pe.wait_ge(sem("at_kept"), n * 8 + (h + 1))
                    for j in range(NCH):
                        last = nc.tensor.transpose(at_turn[j // 3][:, (j % 3) * 128:(j % 3) * 128 + 128],
                                                   pr[h % 2][0][:, 128 * j:128 * j + 128], C("ident"))
                    last.then_inc(sem("at_turn"), 1)
                    if h < 6:
                        scores(h + 2)
                    pe.wait_ge(sem("at_turned"), n * 8 + (h + 1))
                    for j in range(NCH):
                        last = nc.tensor.matmul(at_turn[0][:, 0:128], vtok[:, j, 128 * h:128 * h + 128], wtt[:, j, :],
                                                start=j == 0, stop=j == NCH - 1)
                    last.then_inc(sem("at_out"), 1)
            head_norm(40, 4, C("mean128"), ONLY_LAT, sqa)
            pe.wait_ge(sem("hn_out"), 2 + 48)
            lin_octet(O_DAOUT, LIN1, ONLY_LAT)
            norm(3, ONLY_LAT)
            peer(1, ONLY_LAT)

        @block.scalar
        def _(act):
            step = Steps(act, "act_step")

            def high(o, i):
                act.wait_ge(w_ready[i % 8], o * 16 + (16 + 16 * (i // 8) - 16 * O_DN))
                nc.scalar.copy(wH[:, i % 2, :, :], raw[:, i % 4, :, :]).then_inc(w_high, 1)

            def used(o, i, ahead=True):
                act.wait_ge(tile_done, o * 8 + (i + 1 - ADA))
                if ahead:
                    high(o, i + 2)

            def norm(q, segs, h_count):
                t0 = segs[0][0]
                nc.scalar.preload_act_table_set("natural_log_exp_and_others")
                if h_count:
                    act.wait_ge(sem("h_done"), h_count)
                for kc in range(KC):
                    nc.scalar.activation(nT[:, kc, t0:T], hT[:, kc, t0:T], ACT.Square).then_inc(sem("norm_sq"), 1)
                act.wait_ge(sem("norm_sum"), q + 1)
                for k, (a, w) in enumerate(segs):
                    last = nc.scalar.activation(nrt[:, a:a + w], aux[:, k, 0:w], ACT.Ln, bias=eps)
                step(last)
                nc.scalar.activation(nrt[:, t0:T], nrt[:, t0:T], ACT.Exp, scale=-0.5).then_inc(sem("norm_root"), 1)
                for kc in range(KC):
                    act.wait_ge(sem("norm_scaled"), 8 * q + kc + 1)
                    for k, (a, w) in enumerate(segs):
                        c = 0 if a == CTX else 1
                        nc.scalar.activation(aH[:, kc, a:a + w], nT[:, kc, a:a + w], ACT.Identity,
                                             bias=mod[:, 48 * (q // 2) + 24 * (q % 2) + kc, c:c + 1])\
                            .then_inc(sem("norm_high"), 2 // len(segs))

            def copy_octets(o0, n, to, segs):
                with act.Fori(0, n) as m:
                    for i in range(8):
                        used(m + o0, i)
                        for k, (a, w) in enumerate(segs):
                            last = nc.scalar.copy(to(m, i)[:, :, a:a + w], lin[:, 2 * (i % 2) + k, 0:w].unsqueeze(1))
                        last.then_inc(lin_free, 1)

            def peer(L, segs):
                o_wq, o_u, o_v, nt, u0, off = peer_shape(L)
                t0 = segs[0][0]
                act.dma_start(keys, io["keys"][L]).then_inc(sem("keys_ready"), 16)
                copy_octets(o_wq, 2, lambda m, i: pqT[:, ds(m * 8 + i, 1), :], segs)
                act.wait_ge(lin_free, 8 * (o_wq + 2) + off + 2)

                def gelu(u, i):
                    o = u + o_u
                    used(o, i)
                    act.wait_ge(sem(f"h_stored{i % 2}"), u * 64 + 16 * (64 * L + i // 2 + 1))
                    for k, (a, w) in enumerate(segs):
                        last = nc.scalar.activation(gl[i % 2][:, a:a + w], lin[:, 2 * (i % 2) + k, 0:w], ACT.Gelu)
                    last.then_inc(lin_free, 1)
                    act.wait_ge(lin_free, o * 8 + (i + 3 + off))
                    act.dma_start(gelu_dram[ds(u * 8 + i, 1), :, t0:T].rearrange("o p n -> (o p) n"),
                                  gl[i % 2][:, t0:T]).then_inc(sem(f"h_stored{i % 2}"), 16)

                with act.Fori(0, nt) as n:
                    step.restart()
                    nc.scalar.copy(qs, pqT[:, :, ds(n * 128 + t0, 128)]).then_inc(sem("tk_query"), 1)
                    act.wait_ge(sem("tk_scores"), n + (u0 + 1))
                    nc.scalar.copy(sc.rearrange("p m n -> p (m n)"), aux[:, :, :].rearrange("p b n -> p (b n)"))\
                        .then_inc(sem("tk_kept"), 1)
                    for i in range(6):
                        gelu(n, i)
                    act.wait_ge(sem("tk_shifted"), n + (u0 + 1))
                    nc.scalar.activation(chosen[2], chosen[2], ACT.Exp).then_inc(sem("tk_exp"), 1)
                    for i in range(6, 8):
                        gelu(n, i)
                    act.wait_ge(sem("tk_turned"), n + (u0 + 1))
                    step(nc.scalar.copy(idx[:, :, ds(n * 128, 128)], aux[:, 0, 0:384].rearrange("p (k n) -> p k n", k=3)))
                step.restart()
                act.sem_inc(sem("idx_ready"), 1)
                q0 = 32 * u0
                with act.Fori(0, 8) as n:
                    for i in range(8):
                        gelu(n + nt, i)
                        for q in range(nt * i // 2, nt * (i + 1) // 2):
                            m, b = q // 4, q // 4 % 2
                            if q % 4 == 0:
                                act.wait_ge(sem(f"gb_stored{b}"), n * (8 * nt) + 16 * (4 * u0 + m // 2 + 1))
                            act.wait_ge(sem("gb_sum"), n * (4 * nt) + (q0 + q + 5))
                            out = stage[b].rearrange("p (g t c) -> p t g c", g=NG, c=8)
                            nc.scalar.copy(out[:, 4 * (q % 4):4 * (q % 4) + 4, :, :],
                                           aux[:, q % 4, :].rearrange("p (t g c) -> p t g c", t=4, c=8))\
                                .then_inc(sem("gb_kept"), 1)
                            if q % 4 == 3:
                                act.wait_ge(sem("gb_kept"), n * (4 * nt) + (q0 + q + 5))
                                act.dma_start(gate_dram[:, :, ds(n * (128 * nt) + (8 * TB * m + 8 * t0), 8 * TB)]
                                              .rearrange("g p x -> p g x"),
                                              stage[b].rearrange("p (g x) -> p g x", g=NG)).then_inc(sem(f"gb_stored{b}"), 16)
                for b in range(2):
                    act.wait_ge(sem(f"gb_stored{b}"), 16 * (4 * (u0 + nt) + 1))

                def load_gates(g, b):
                    act.dma_start(ggate[b][:, t0:T, :].rearrange("p n c -> p (n c)"),
                                  gate_dram[ds(g, 1), :, 8 * t0:8 * T].rearrange("o p x -> (o p) x"))\
                        .then_inc(sem(f"gg_ready{b}"), 16)

                def load_gelu(c, b):
                    act.dma_start(hb[b][:, t0:T], gelu_dram[ds(c, 1), :, t0:T].rearrange("o p n -> (o p) n"))\
                        .then_inc(sem(f"hb_ready{b}"), 16)

                def product(c, i, ahead):
                    act.wait_ge(sem("p_mul"), c + (128 * L + 1))
                    nc.scalar.copy(prodH[:, i // 4, i % 4, t0:T], hb[i % 2][:, t0:T]).then_inc(sem("p_high"), 1)
                    if ahead:
                        act.wait_ge(sem("p_done"), c + (128 * L + 1))
                        load_gelu(c + 2, i % 2)

                def v_octet(v, b, last=2):
                    o = v + o_v
                    for i in range(8):
                        if last or i < 4:
                            act.wait_ge(tile_done, o * 8 + (4 * (i // 4) - ADA))
                            product(v * 8 + (i + 4), (i + 4) % 8, last or i < 2)
                        if i == 3 and last == 2:
                            load_gates(v + 2, b)
                        used(o, i, L == 0 or last or i < 6)

                load_gates(0, 0)
                load_gates(1, 1)
                load_gelu(0, 0)
                load_gelu(1, 1)
                with act.Fori(nt + 8, 15) as u:
                    for i in range(8):
                        gelu(u, i)
                for i in range(4):
                    product(i, i, True)
                    gelu(15, i)
                for i in range(4, 8):
                    gelu(15, i)
                act.sem_inc(sem("u_read"), 1)
                for b in range(2):
                    act.wait_ge(sem(f"h_stored{b}"), 16 * (64 * (L + 1) + 1))
                with act.Fori(0, 7) as n:
                    for b in range(2):
                        v_octet(n * 2 + b, b)
                v_octet(14, 0, 1)
                v_octet(15, 1, 0)

            def head_norm(base, iters, src, segs, e, sq=sq, rt=rt, split=False):
                t0 = segs[0][0]
                nc.scalar.preload_act_table_set("natural_log_exp_and_others")
                with act.Fori(0, iters) as n:
                    step.restart()
                    for b in range(2):
                        act.wait_ge(sem("hn_sum"), n * 2 + (base + b + 1))
                        if split:
                            act.wait_ge(sem("hn_out"), n * 2 + (base + b + 1))
                        nc.scalar.activation(sq[b][:, t0:T], src(n, b)[:, t0:T], ACT.Square).then_inc(sem("hn_sq"), 1)
                    for b in range(2):
                        act.wait_ge(sem("hn_sum"), n * 2 + (base + b + 3))
                        act.wait_ge(sem("hn_out"), n * 2 + (base + b + 1))
                        for k, (a, w) in enumerate(segs):
                            last = nc.scalar.activation(rt[b][:, a:a + w], aux[:, 2 * b + k, 0:w], ACT.Ln, bias=e)
                        step.mark(last)
                    step.wait()
                    for b in range(2):
                        nc.scalar.activation(rt[b][:, t0:T], rt[b][:, t0:T], ACT.Exp, scale=-0.5).then_inc(sem("hn_root"), 1)

            act.sem_inc(lin_free, 2)
            act.sem_inc(sem("ada_row"), 3)
            for x in ("conv_done", "silu_done", "hn_sum", "hn_root", "hn_out"):
                act.sem_inc(sem(x), 2)
            act.sem_inc(sem("rope_done"), 2)
            act.sem_inc(sem("at_exp"), 2)
            for x in ("at_kept", "at_used"):
                act.sem_inc(sem(x), 1)
            act.sem_inc(sem("gb_kept"), 4)
            act.sem_inc(sem("gb_sum"), 4)
            for b in range(2):
                act.sem_inc(sem(f"gb_stored{b}"), 16)
                act.sem_inc(sem(f"h_stored{b}"), 16)
            for x in ("bank_read00", "bank_read01", "bank_read10", "bank_read11"):
                act.sem_inc(sem(x), 1)
            act.wait_ge(sem("params_ready"), 16)
            nc.scalar.activation(cond, cond, ACT.Silu).then_inc(sem("cond_ready"), 1)
            ada_loads(act, 1)
            act.wait_ge(sem("x_ready"), 16)
            act.wait_ge(sem("eps_ready"), 1)
            act.wait_ge(sem("mod_ready"), 1)
            for i in range(2):
                high(O_DN, i)
            norm(0, ALL, 0)
            act.wait_ge(sem("pads_ready"), 1)

            with act.Fori(0, 3) as n:
                def silu(i):
                    b = i % 2
                    act.wait_ge(sem("conv_done"), n * 8 + (i + 3))
                    nc.scalar.activation(qkvT[:, ds(n * 8 + i, 1), 0:CTX], co[b][:, 0:CTX].unsqueeze(1), ACT.Silu)
                    nc.scalar.activation(qkvT[:, ds(n * 8 + i, 1), CTX:T], co[b][:, CTX + 4:T + 4].unsqueeze(1), ACT.Silu)\
                        .then_inc(sem("silu_done"), 1)
                for i in range(8):
                    b = i % 2
                    used(n + O_DN, i)
                    act.wait_ge(sem("conv_done"), n * 8 + (i + 1))
                    nc.scalar.copy(xp[b][:, 2:2 + CTX], lin[:, 2 * b, 0:CTX])
                    nc.scalar.copy(xp[b][:, 6 + CTX:6 + T], lin[:, 2 * b + 1, :]).then_inc(lin_free, 1)
                    if i:
                        silu(i - 1)
                silu(7)
            for i in range(8):
                used(O_DN + 3, i)
                nc.scalar.activation(zT[:, i, 0:CTX], lin[:, 2 * (i % 2), 0:CTX], ACT.Silu)
                nc.scalar.activation(zT[:, i, CTX:T], lin[:, 2 * (i % 2) + 1, :], ACT.Silu).then_inc(lin_free, 1)
            act.wait_ge(sem("gate_sum"), 1)
            ab = aux[:, 2, 0:192].rearrange("p (c k n) -> p c k n", c=NCH, k=2)
            nc.scalar.activation(beta, ab[:, :, 0, :], ACT.Sigmoid).then_inc(sem("beta_ready"), 1)
            step(nc.scalar.activation(a_log, a_log, ACT.Exp))
            act.wait_ge(sem("gate_abs"), 1)
            step(nc.scalar.activation(gtmp[:, 96:192], gtmp[:, 96:192], ACT.Exp, scale=-1.0))
            nc.scalar.activation(gtmp[:, 96:192], gtmp[:, 96:192], ACT.Ln, bias=1.0).then_inc(sem("gate_ln"), 1)
            act.wait_ge(sem("gate_tot"), 1)
            act.wait_ge(sem("gate_diff"), 1)
            nc.scalar.activation(kdf, kdf, ACT.Exp)
            nc.scalar.activation(dec.rearrange("p c n -> p (c n)"), aux[:, 3, 128:224], ACT.Exp)
            nc.scalar.activation(negE, negG, ACT.Exp, scale=-1.0).then_inc(sem("gates_exp"), 1)
            act.wait_ge(sem("gates_done"), 1)
            head_norm(0, 8, lambda n, b: qkvT[:, ds(n + 8 * b, 1), :].rearrange("p o n -> p (o n)"), ALL, eps)

            def delta(n, chunk):
                for hg in range(2):
                    for d in range(2):
                        act.wait_ge(sem(f"diff_done{d}"), n * 2 + hg + 1)
                        nc.scalar.activation(egq[d], lin[:, 2 * d, :].rearrange("p (h n) -> p h n", n=128), ACT.Exp)\
                            .then_inc(sem(f"bank_read{d}0"), 1)
                    for d in range(2):
                        nc.scalar.activation(Em[d], Em[d], ACT.Exp).then_inc(sem(f"pair_decay{d}"), 1)
                    for d in range(2):
                        act.wait_ge(sem(f"bank_full{d}0"), n * (2 * USES[0]) + hg * USES[0] + 2)
                        nc.scalar.copy(vt[d], lin[:, 2 * d, :].rearrange("p (h n) -> p h n", n=128))\
                            .then_inc(sem(f"bank_read{d}0"), 1)

            with act.Fori(0, 2) as n:
                delta(n, [n, act.snap(n * (-1) + 1)])
            with act.Fori(2, NCH) as n:
                delta(n, [n, act.snap(n * (-1) + 7)])
            act.wait_ge(sem("delta_done"), 1)
            act.dma_start(hT[:, :, :], io["x"]).then_inc(sem("x_ready"), 16)
            head_norm(16, 4, lambda n, b: oT[:, ds(n * 2 + b, 1), :].rearrange("p o n -> p (o n)"), ALL, eps, sq2, rt2, True)
            for i in range(8):
                used(O_DNOUT, i)
            step.restart()
            norm(1, ALL, 1)
            act.wait_ge(sem("norm_done"), 32)
            peer(0, ALL)
            norm(2, ALL, 2)
            act.dma_start(rope, io["rope"]).then_inc(sem("rope_ready"), 16)
            act.dma_start(lamv.rearrange("p a b n -> p (a b n)"), io["lambdas"]).then_inc(sem("lambdas_ready"), 16)
            copy_octets(O_QKV, 1, lambda m, i: qT[:, i:i + 1, :], ONLY_LAT)
            copy_octets(O_QKV + 1, 1, lambda m, i: kT[:, i:i + 1, :], ALL)
            for i in range(8):
                used(O_QKV + 2, i)
                for k in range(2):
                    last = nc.scalar.copy(vtok[:, 3 * k:3 * k + 3, 128 * i:128 * i + 128],
                                          lin[:, 2 * (i % 2) + k, 0:384].rearrange("p (t n) -> p t n", t=3))
                last.then_inc(lin_free, 1)
            act.wait_ge(sem("lam_sums"), 1)
            nc.scalar.activation(lam[:, 0:2], lam[:, 0:2], ACT.Exp).then_inc(sem("lam_exp"), 1)
            act.wait_ge(lin_free, 8 * (O_QKV + 3) + LIN1 + 2)
            one = lambda x, n, b: x[:, ds(n * 2 + b, 1), :].rearrange("p o n -> p (o n)")
            head_norm(24, 4, lambda n, b: one(qT, n, b), ONLY_LAT, eps, sqa, rta)
            head_norm(32, 4, lambda n, b: one(kT, n, b), ALL, eps, sqa, rta)
            with act.Fori(0, LAT // 128) as n:
                def exps(h):
                    act.wait_ge(sem("at_max"), n * 8 + (h + 1))
                    for c in range(2):
                        last = nc.scalar.activation(pr[h % 2][c], at_scores[h % 2][:, T * c:T * c + T], ACT.Exp,
                                                    bias=mx[:, 4 * (h % 2) + 2 + c:4 * (h % 2) + 3 + c],
                                                    accum_out=mx[:, 8 + 4 * (h % 2) + c:9 + 4 * (h % 2) + c])
                    last.then_inc(sem("at_exp"), 1)
                exps(0)
                exps(1)
                for h in range(8):
                    act.wait_ge(sem("at_turn"), n * 8 + (h + 1))
                    for k in range(2):
                        last = nc.scalar.copy(wtt[:, 3 * k:3 * k + 3, :].rearrange("p t n -> p (t n)"), at_turn[k][:, 0:384])
                    last.then_inc(sem("at_turned"), 1)
                    if h < 6:
                        exps(h + 2)
            act.wait_ge(sem("at_kept"), 33)
            head_norm(40, 4, lambda n, b: one(oT, n, b), ONLY_LAT, eps, sqa, rta, True)
            for i in range(8):
                used(O_DAOUT, i)
            step.restart()
            norm(3, ONLY_LAT, 3)
            act.wait_ge(sem("norm_done"), 64)
            peer(1, ONLY_LAT)

        @block.gpsimd
        def _(pool):
            step = Steps(pool, "pool_step")
            def low_parts(o0, o1):
                with pool.Fori(o0, o1) as o:
                    for i in range(8):
                        pool.wait_ge(w_high, o * 8 + (i + 1 - ADA))
                        nc.gpsimd.tensor_tensor(wL[:, i % 2, :, :], raw[:, i % 4, :, :], wH[:, i % 2, :, :].bitcast(F32),
                                                ALU.subtract).then_inc(raw_used, 1)

            nc.gpsimd.memset(eps, EPS).then_inc(sem("eps_ready"), 1)
            pool.wait_ge(sem("norm_scaled"), 8)
            nc.gpsimd.memset(hflat[:, 0:2 * XPW], 0.0).then_inc(sem("pads_ready"), 1)
            low_parts(O_DN, O_DNOUT)
            pool.wait_ge(sem("hn_out"), 2 + 16)
            for x in state:
                nc.gpsimd.memset(x, 0.0).then_inc(sem("state_zero"), 1)
            nc.gpsimd.memset(oT[:, :, :], 0.0).then_inc(sem("o_zero"), 1)

            def delta(n, chunk):
                for hg in range(2):
                    for d in range(2):
                        H = slice(4 * hg, 4 * hg + 4)
                        pool.wait_ge(sem(f"state_ready{d}"), n * 2 + hg + 1)
                        nc.gpsimd.tensor_copy(gby[d], cols(g_[:, ds(chunk[d], 1), 8 * d + 4 * hg:8 * d + 4 * hg + 4]
                                              .rearrange("p o n -> p (o n)"))).then_inc(sem(f"staged{d}"), 1)
                        c = ds(chunk[d] * 128, 128)
                        nc.gpsimd.tensor_copy(kts[d], qkvT[:, 8 + 4 * hg:12 + 4 * hg, c])
                        nc.gpsimd.tensor_copy(vts[d], qkvT[:, 16 + 4 * hg:20 + 4 * hg, c]).then_inc(sem(f"staged{d}"), 1)
                    for d in range(2):
                        pool.wait_ge(sem(f"bank_read{d}0"), n * (2 * USES[0]) + hg * USES[0] + 2)
                        c = ds(chunk[d] * 128, 128)
                        nc.gpsimd.tensor_tensor(egq[d], egq[d], qkvT[:, 4 * hg:4 * hg + 4, c], ALU.mult)\
                            .then_inc(sem(f"q_decayed{d}"), 1)

            with pool.Fori(0, 2) as n:
                delta(n, [n, pool.snap(n * (-1) + 1)])
            with pool.Fori(2, NCH) as n:
                delta(n, [n, pool.snap(n * (-1) + 7)])
            low_parts(O_DNOUT, O_DAOUT)
            with pool.Fori(0, LAT // 128) as n:
                pool.wait_ge(sem("rope_done"), 18)
                pool.wait_ge(sem("at_used"), n + 1)
                nc.gpsimd.tensor_copy(qst, qT[:, :, ds(n * 128 + CTX, 128)]).then_inc(sem("at_query"), 1)
            low_parts(O_DAOUT, O_END)

        @block.vector
        def _(dve):
            step = Steps(dve, "dve_step")
            V = nc.vector

            def norm(q, segs):
                dve.wait_ge(sem("norm_root"), q + 1)
                for kc in range(KC):
                    for k, (a, w) in enumerate(segs):
                        c = 0 if a == CTX else 1
                        last = V.scalar_tensor_tensor(nT[:, kc, a:a + w], hT[:, kc, a:a + w], gsc[:, q, kc, c:c + 1],
                                                      nrt[:, a:a + w], ALU.mult, ALU.mult)
                    last.then_inc(sem("norm_scaled"), 1)
                for kc in range(KC):
                    for k, (a, w) in enumerate(segs):
                        c = 0 if a == CTX else 1
                        dve.wait_ge(sem("norm_high"), 16 * q + 2 * kc + 1 + (k if len(segs) > 1 else 1))
                        V.scalar_tensor_tensor(aL[:, kc, a:a + w], nT[:, kc, a:a + w],
                                               mod[:, 48 * (q // 2) + 24 * (q % 2) + kc, c:c + 1],
                                               aH[:, kc, a:a + w].bitcast(F32), ALU.add, ALU.subtract)\
                            .then_inc(sem("norm_done"), 2 // len(segs))

            def head_norm(base, iters, src, segs, gain, gate=None, rt=rt, sq=sq, split=False):
                t0 = segs[0][0]
                with dve.Fori(0, iters) as n:
                    step.restart()
                    for b in range(2):
                        dve.wait_ge(sem("hn_root"), n * 2 + (base + b + 3))
                        x = src(n, b)[:, t0:T]
                        out = sq[b][:, t0:T] if split else x
                        ins = V.scalar_tensor_tensor(out, x, gain(b), rt[b][:, t0:T], ALU.mult, ALU.mult)
                        if gate:
                            step(ins)
                            ins = V.tensor_tensor(out, out, gate(n, b)[:, t0:T], ALU.mult)
                        if split:
                            step(ins)
                            high, low = (x[:, ds(n * 2 + b, 1), t0:T].rearrange("p o n -> p (o n)") for x in (aH, aL))
                            step(V.tensor_copy(high, sq[b][:, t0:T]))
                            ins = V.tensor_tensor(low, sq[b][:, t0:T], high.bitcast(F32), ALU.subtract)
                        ins.then_inc(sem("hn_out"), 1)
                step.restart()

            for o in range(O_DN):
                dve.wait_ge(sem("ada_used"), o + 1)
                V.tensor_copy(ada_rows[0:2, 1024 * o:1024 * o + 1024].rearrange("p (k n) -> p k n", k=2), ada_sum[o % 3])\
                    .then_inc(sem("ada_row"), 1)
            dve.wait_ge(sem("ada_turned"), 1)
            dve.wait_ge(sem("params_ready"), 16)
            V.tensor_tensor(mod[:, :, :], aux[:, 0, 0:192].rearrange("p (t c) -> p t c", c=2), cols(ada_b, 2),
                            ALU.add).then_inc(sem("ada_read"), 1)
            dve.wait_ge(sem("ada_read"), 1)
            for q in range(4):
                a = 48 * (q // 2) + 24 * (q % 2) + 8
                ins = V.scalar_tensor_tensor(gsc[:, q, :, :], mod[:, a:a + 8, :], 1.0, cols(norm_g[:, 8 * q:8 * q + 8], 2),
                                             ALU.add, ALU.mult)
                step(ins)
            dve.sem_inc(sem("mod_ready"), 1)
            norm(0, ALL)

            with dve.Fori(0, 3) as n:
                step.restart()
                for i in range(8):
                    b = i % 2
                    dve.wait_ge(lin_free, n * 8 + (i + 3))
                    dve.wait_ge(sem("silu_done"), n * 8 + (i + 1))
                    w = [conv_w[:, ds(n * 40 + (5 * i + k), 1)] for k in range(5)]
                    W = T + 4
                    step(V.tensor_scalar(co[b][:, 0:W], xp[b][:, 0:W], w[0], None, ALU.mult))
                    for k in range(1, 5):
                        ins = V.scalar_tensor_tensor(co[b][:, 0:W], xp[b][:, k:k + W], w[k], co[b][:, 0:W],
                                                     ALU.mult, ALU.add)
                        if k < 4:
                            step(ins)
                    ins.then_inc(sem("conv_done"), 1)
            step.restart()
            dve.wait_ge(sem("beta_ready"), 1)
            ab = aux[:, 2, 0:192].rearrange("p (c k n) -> p c k n", c=NCH, k=2)
            x3 = gtmp[:, 0:96].rearrange("p (c n) -> p c n", n=16)
            step(V.tensor_tensor(x3, ab[:, :, 1, :], dt_bias.unsqueeze(1).to_broadcast([128, NCH, 16]), ALU.add))
            V.scalar_tensor_tensor(gtmp[:, 96:192], gtmp[:, 0:96], -1.0, gtmp[:, 0:96], ALU.mult, ALU.max)\
                .then_inc(sem("gate_abs"), 1)
            dve.wait_ge(sem("gate_ln"), 1)
            step(V.scalar_tensor_tensor(gtmp[:, 0:96], gtmp[:, 0:96], 0.0, gtmp[:, 96:192], ALU.max, ALU.add))
            V.scalar_tensor_tensor(g_, x3, -1.0, a_log.unsqueeze(1).to_broadcast([128, NCH, 16]), ALU.mult, ALU.mult)\
                .then_inc(sem("gate_ready"), 1)
            dve.wait_ge(sem("gate_tot"), 1)
            step(V.tensor_scalar(negG.rearrange("p c n -> p (c n)"), aux[:, 3, 0:96], -1.0, None, ALU.mult))
            V.tensor_tensor(kdf.rearrange("p c n -> p (c n)"), aux[:, 3, 128:224], negG.rearrange("p c n -> p (c n)"),
                            ALU.add).then_inc(sem("gate_diff"), 1)
            dve.wait_ge(sem("gates_exp"), 1)
            V.tensor_scalar(negE, negE, -1.0, None, ALU.mult).then_inc(sem("gates_done"), 1)
            head_norm(0, 8, lambda n, b: qkvT[:, ds(n + 8 * b, 1), :].rearrange("p o n -> p (o n)"), ALL,
                      lambda b: 128 ** -0.5 if b == 0 else 1.0)

            P = [[lin[:, 2 * d + k, :].rearrange("p (h n) -> p h n", n=128) for k in range(2)] for d in range(2)]
            TT = V.tensor_tensor
            dve.wait_ge(sem("state_zero"), 4)
            dve.wait_ge(sem("o_zero"), 1)
            for d in range(2):
                dve.sem_inc(sem(f"state_ready{d}"), 1)

            def delta(n, chunk):
                step.restart()
                for hg in range(2):
                    use = [[0, 0], [0, 0]]

                    def full(d, k):
                        use[d][k] += 1
                        dve.wait_ge(sem(f"bank_full{d}{k}"), n * (2 * USES[k]) + hg * USES[k] + use[d][k])
                        return P[d][k]

                    def read(d, k, ins):
                        ins.then_inc(sem(f"bank_read{d}{k}"), 1)

                    def gate(x, d):
                        return cols(x[:, ds(chunk[d], 1), 8 * d + 4 * hg:8 * d + 4 * hg + 4]
                                    .rearrange("p o n -> p (o n)"))

                    for d in range(2):
                        step(TT(Em[d], full(d, 0), gate(negG, d), ALU.add))
                        V.tensor_scalar(Em[d], Em[d], 0.0, None, ALU.min).then_inc(sem(f"diff_done{d}"), 1)
                    for d in range(2):
                        use[d][0] += 1
                        dve.wait_ge(sem(f"pair_decay{d}"), n * 2 + hg + 1)
                        step.mark(TT(Em[d], Em[d], heads4(C(f"until{d}")), ALU.mult))
                    step.wait()
                    for d in range(2):
                        step.mark(TT(eb[d], Em[d], gate(beta, d), ALU.mult))
                    step.wait()
                    for d in range(2):
                        step.mark(TT(AT[d], full(d, 1), eb[d], ALU.mult))
                    step.wait()
                    for d in range(2):
                        dve.sem_inc(sem(f"bank_read{d}1"), 1)
                        step.mark(TT(Um[d], AT[d], heads4(C(f"level{1 - d}_0")), ALU.mult))
                    step.wait()
                    for d in range(2):
                        step.mark(TT(Um[d], heads4(C("ident")), Um[d], ALU.subtract))
                    step.wait()
                    for d in range(2):
                        read(d, 1, TT(Em[d], full(d, 1), Em[d], ALU.mult))
                    for d in range(2):
                        step.mark(TT(Tm[d], full(d, 0), heads4(C(f"level{d}_0")), ALU.mult))
                    step.wait()
                    for d in range(2):
                        dve.sem_inc(sem(f"bank_read{d}0"), 1)
                        TT(Tm[d], heads4(C("ident")), Tm[d], ALU.subtract).then_inc(sem(f"inverse{d}"), 1)
                    for lv in range(1, 7):
                        for d in range(2):
                            read(d, 0, TT(gby[d], full(d, 0), heads4(C(f"level{d}_{lv}")), ALU.mult))
                        for d in range(2):
                            if lv < 6:
                                x = full(d, 1)
                                t = half(Tm[d], lv, d)
                                read(d, 1, TT(t, t, half(x, lv, d), ALU.subtract))
                            x = full(d, 0)
                            t = half(Um[d], lv, 1 - d)
                            read(d, 0, TT(t, t, half(x, lv, 1 - d), ALU.subtract))
                    for d in range(2):
                        step.mark(TT(eb[d], full(d, 1), gate(negE, d), ALU.mult))
                    step.wait()
                    for d in range(2):
                        read(d, 1, TT(eb[d], eb[d], vt[d], ALU.add))
                    for d in range(2):
                        read(d, 0, TT(kts[d], full(d, 0), gate(kdf, d), ALU.mult))
                    for d in range(2):
                        read(d, 1, TT(dl[d], full(d, 1), gate(beta, d), ALU.mult))
                        st = state[2 * hg + d]
                        step(TT(vts[d], st, gate(dec, d), ALU.mult))
                    for d in range(2):
                        o = oT[:, 4 * hg:4 * hg + 4, ds(chunk[d] * 128, 128)]
                        x = full(d, 0)
                        read(d, 0, TT(o, x, o, ALU.add))
                        x = full(d, 1)
                        step(TT(state[2 * hg + d], x, vts[d], ALU.add))
                        dve.sem_inc(sem(f"bank_read{d}1"), 1)
                        dve.sem_inc(sem(f"state_ready{d}"), 1)
                    assert [use[d][k] for d in range(2) for k in range(2)] == [USES[0], USES[1]] * 2, use

            with dve.Fori(0, 2) as n:
                delta(n, [n, dve.snap(n * (-1) + 1)])
            with dve.Fori(2, NCH) as n:
                delta(n, [n, dve.snap(n * (-1) + 7)])
            step.restart()
            dve.sem_inc(sem("delta_done"), 1)
            head_norm(16, 4, lambda n, b: oT[:, ds(n * 2 + b, 1), :].rearrange("p o n -> p (o n)"), ALL,
                      lambda b: dn_g, lambda n, b: zT[:, ds(n * 2 + b, 1), :].rearrange("p o n -> p (o n)"),
                      rt2, sq2, True)

            def residual(o, segs, gate_at):
                for i in range(8):
                    dve.wait_ge(tile_done, 8 * o + i + 1 - ADA)
                    for k, (a, w) in enumerate(segs):
                        c = 0 if a == CTX else 1
                        ins = V.scalar_tensor_tensor(hT[:, i, a:a + w], lin[:, 2 * (i % 2) + k, 0:w],
                                                     mod[:, gate_at + i, c:c + 1], hT[:, i, a:a + w], ALU.mult, ALU.add)
                    step(ins)
                    dve.sem_inc(lin_free, 1)
                dve.sem_inc(sem("h_done"), 1)

            dve.wait_ge(sem("x_ready"), 32)
            residual(O_DNOUT, ALL, 16)

            def peer(L, segs):
                o_wq, o_u, o_v, nt, u0, off = peer_shape(L)
                t0 = segs[0][0]
                with dve.Fori(0, nt) as n:
                    step.restart()
                    dve.wait_ge(sem("tk_kept"), n + (u0 + 1))
                    V.memset(gsum[:, 8:9], 0.0)
                    for m in range(16):
                        step.mark(V.max(tv[:, m, 0:8], sc[:, m, :]))
                    step.wait()
                    for m in range(16):
                        step.mark(V.max_index(ti[:, m, 0:8], tv[:, m, 0:8], sc[:, m, :]))
                        step.mark(V.match_replace(sc2[:, m, :], tv[:, m, 0:8], sc[:, m, :], -3.0e38))
                    step.wait()
                    for m in range(16):
                        step.mark(V.max(tv[:, m, 8:16], sc2[:, m, :]))
                    step.wait()
                    for m in range(16):
                        step.mark(V.max_index(ti[:, m, 8:16], tv[:, m, 8:16], sc2[:, m, :]))
                    step.wait()
                    step.mark(V.tensor_copy(tf, ti))
                    halves = tv.rearrange("p (h s) n -> p h s n", s=2)
                    for h in range(HEADS):
                        step.mark(TT(cand[:, h, :].rearrange("p (a b) -> p a b", a=16),
                                     halves[:, h, 0, :].unsqueeze(2).to_broadcast([128, 16, 16]),
                                     halves[:, h, 1, :].unsqueeze(1).to_broadcast([128, 16, 16]), ALU.add))
                    step.wait()
                    for h in range(HEADS):
                        step.mark(V.max(best[:, h, 0:8], cand[:, h, :]))
                    step.wait()
                    for h in range(HEADS):
                        step.mark(V.max_index(bpos[:, h, 0:8], best[:, h, 0:8], cand[:, h, :]))
                        step.mark(V.match_replace(cand2[:, h, :], best[:, h, 0:8], cand[:, h, :], -3.0e38))
                    step.wait()
                    for h in range(HEADS):
                        step.mark(V.max(best[:, h, 8:16], cand2[:, h, :]))
                    step.wait()
                    for h in range(HEADS):
                        step.mark(V.max_index(bpos[:, h, 8:16], best[:, h, 8:16], cand2[:, h, :]))
                    gate3 = chosen[2].rearrange("p (h n) -> p h n", n=16)
                    TT(gate3, best, best[:, :, 0:1].to_broadcast([128, 8, 16]), ALU.subtract).then_inc(sem("tk_shifted"), 1)
                    step.wait()
                    flat = bpos.rearrange("p h n -> p (h n)")
                    step.mark(V.tensor_scalar(posi[0], flat, 4, None, ALU.logical_shift_right))
                    step.mark(V.tensor_scalar(posi[1], flat, 15, None, ALU.bitwise_and))
                    step.wait()
                    for k in range(2):
                        step.mark(V.tensor_copy(posf[k], posi[k]))
                    step.wait()
                    eq3 = eq.rearrange("p (m a) -> p m a", a=16)
                    for k in range(2):
                        step(TT(eq3, cols(posf[k], 16), C("iota")[:, 0:16].unsqueeze(1).to_broadcast([128, 128, 16]),
                                ALU.is_equal))
                        pick = tf.rearrange("p (h s) a -> p h s a", s=2)[:, :, k, :]
                        step(TT(eq.rearrange("p (h m a) -> p h m a", h=8, a=16), eq.rearrange("p (h m a) -> p h m a", h=8, a=16),
                                pick.unsqueeze(2).to_broadcast([128, 8, 16, 16]), ALU.mult))
                        step(V.reduce_sum(chosen[k], eq3, AX.X))
                    dve.wait_ge(sem("tk_exp"), n + (u0 + 1))
                    step(V.reduce_sum(gsum[:, 0:8], gate3, AX.X))
                    step(V.reciprocal(gsum[:, 0:8], gsum[:, 0:8]))
                    TT(gate3, gate3, cols(gsum[:, 0:8], 16), ALU.mult).then_inc(sem("tk_chosen"), 1)
                step.restart()
                q0 = 32 * u0
                dve.wait_ge(sem("idx_ready"), L + 1)
                with dve.Fori(0, 8) as n:
                    step.restart()
                    NT = 16 * nt
                    step(V.tensor_copy(bidx[:, 0:3, 0:NT], idx[:, :, ds(n * NT, NT)]))
                    step(V.tensor_copy(bhigh[:, 0:NT], bidx[:, 2, 0:NT]))
                    step(TT(bidx[:, 3, 0:NT], bidx[:, 2, 0:NT], bhigh[:, 0:NT].bitcast(F32), ALU.subtract))
                    for q in range(4 * nt):
                        dve.wait_ge(sem("gb_sum"), n * (4 * nt) + (q0 + q + 1))
                        for t in range(4):
                            k, c = 4 * (q % 4) + t, 4 * q + t
                            V.tensor_scalar(hot[0][:, k, :], C("iota"), bidx[:, 0, c:c + 1], None, ALU.is_equal)
                            for j, gate in ((1, bhigh[:, c:c + 1].bitcast(F32)), (2, bidx[:, 3, c:c + 1])):
                                last = V.tensor_scalar(hot[j][:, k, :], C("iota"), bidx[:, 1, c:c + 1], gate,
                                                       ALU.is_equal, ALU.mult)
                        last.then_inc(sem("gb_hot"), 1)
                    dve.wait_ge(sem("gb_hot"), n * (4 * nt) + (q0 + 4 * nt))
                step.restart()

                def multiply(v4, i, b):
                    dve.wait_ge(sem(f"hb_ready{i % 2}"), v4 * 64 + 16 * (64 * L + i // 2 + 1))
                    TT(hb[i % 2][:, t0:T], hb[i % 2][:, t0:T], ggate[b][:, t0:T, i % 8], ALU.mult)\
                        .then_inc(sem("p_mul"), 1)

                def low_part(v4, i):
                    dve.wait_ge(sem("p_high"), v4 * 8 + (128 * L + i + 1))
                    place = (slice(None), i // 4 % 2, i % 4, slice(t0, T))
                    TT(prodL[place], hb[i % 2][:, t0:T], prodH[place].bitcast(F32), ALU.subtract)\
                        .then_inc(sem("p_done"), 1)

                offv = LINV1 if L else LINV0

                def gather(o, i, s):
                    m = 2 * (i % 4) + s
                    dve.wait_ge(lin_free, o * 16 + (2 * i + s - 5 + offv))
                    for k, (a, w) in enumerate(segs):
                        c = 0 if a == CTX else 1
                        last = V.scalar_tensor_tensor(hT[:, m, a:a + w], lin[:, 2 * s + k, 0:w],
                                                      mod[:, 48 * L + 40 + m, c:c + 1], hT[:, m, a:a + w],
                                                      ALU.mult, ALU.add)
                    last.then_inc(lin_free, 1)

                def v_octet(v, b, g, last=False):
                    o = v + o_v
                    for i in range(8):
                        if i == 4 and not last:
                            dve.wait_ge(sem(f"gg_ready{1 - b}"), g * 16 + 16 * (8 * L + 1))
                        new = i < 4 or not last
                        if new:
                            multiply(v, i + 4, b if i < 4 else 1 - b)
                        dve.wait_ge(v_half, o * 8 + (i + 1 + 128 * L - 8 * o_v))
                        gather(o, i, 0)
                        if new:
                            low_part(v, i + 4)
                        dve.wait_ge(tile_done, o * 8 + (i + 1 - ADA))
                        gather(o, i, 1)

                dve.wait_ge(sem("gg_ready0"), 16 * (8 * L + 1))
                for i in range(4):
                    multiply(0, i, 0)
                    low_part(0, i)
                dve.wait_ge(sem("u_read"), L + 1)
                with dve.Fori(0, 7) as n:
                    v_octet(n * 2, 0, n)
                    v_octet(n * 2 + 1, 1, n + 1)
                v_octet(14, 0, 7)
                v_octet(15, 1, 8, True)
                dve.wait_ge(lin_free, 16 * (o_v + 16) + offv + 2)
                dve.sem_inc(sem("h_done"), 1)

            norm(1, ALL)
            peer(0, ALL)
            norm(2, ALL)
            dve.wait_ge(sem("lambdas_ready"), 16)
            step(TT(lamv[:, :, 0, :], lamv[:, :, 0, :], lamv[:, :, 1, :], ALU.mult))
            V.reduce_sum(lam[:, 0:2], lamv[:, :, 0, :], AX.X).then_inc(sem("lam_sums"), 1)
            dve.wait_ge(sem("lam_exp"), 1)
            step(TT(lam[:, 2:3], lam[:, 0:1], lam[:, 1:2], ALU.subtract))
            step(V.tensor_scalar(lam[:, 2:3], lam[:, 2:3], LAMBDA_INIT, None, ALU.add))
            step(V.tensor_scalar(da_qg, da_qg, 64 ** -0.5, None, ALU.mult))
            step(V.tensor_scalar(da_sg, da_sg, 1.0 - LAMBDA_INIT, None, ALU.mult))
            one = lambda x, n, b: x[:, ds(n * 2 + b, 1), :].rearrange("p o n -> p (o n)")
            head_norm(24, 4, lambda n, b: one(qT, n, b), ONLY_LAT, lambda b: da_qg, rt=rta)
            head_norm(32, 4, lambda n, b: one(kT, n, b), ALL, lambda b: da_kg, rt=rta)
            dve.wait_ge(sem("hn_out"), 42)
            dve.wait_ge(sem("rope_ready"), 16)
            with dve.Fori(0, 8) as n:
                step.restart()
                for b in range(2):
                    x = (kT if b else qT)[:, ds(n, 1), CTX:T].rearrange("p o n -> p (o n)")
                    step.mark(TT(rtmp[b][0], x, rope[:, 0, :], ALU.mult))
                    dve.wait_ge(sem("rope_turned"), n * 2 + (b + 1))
                    step(TT(rtmp[b][1], aux[:, b, :], rope[:, 1, :], ALU.mult))
                    TT(x, rtmp[b][0], rtmp[b][1], ALU.add).then_inc(sem("rope_done"), 1)
            step.restart()
            with dve.Fori(0, LAT // 128) as n:
                step.restart()

                def maxima(h):
                    dve.wait_ge(sem("at_scores"), n * 8 + (h + 1))
                    m = mx[:, 4 * (h % 2):4 * (h % 2) + 4]
                    for c in range(2):
                        step.mark(V.tensor_reduce(m[:, c:c + 1], at_scores[h % 2][:, T * c:T * c + T], AX.X, ALU.max))
                    step.wait()
                    V.tensor_scalar(m[:, 2:4], m[:, 0:2], -1.0, None, ALU.mult).then_inc(sem("at_max"), 1)

                def weights(h):
                    dve.wait_ge(sem("at_exp"), n * 8 + (h + 3))
                    z = mx[:, 8 + 4 * (h % 2):12 + 4 * (h % 2)]
                    step(V.reciprocal(z[:, 2:4], z[:, 0:2]))
                    step(TT(z[:, 3:4], z[:, 3:4], lam[:, 2:3], ALU.mult))
                    step(V.tensor_scalar(pr[h % 2][1], pr[h % 2][1], z[:, 3:4], None, ALU.mult))
                    V.scalar_tensor_tensor(pr[h % 2][0], pr[h % 2][0], z[:, 2:3], pr[h % 2][1], ALU.mult, ALU.subtract)\
                        .then_inc(sem("at_weights"), 1)
                maxima(0)
                maxima(1)
                weights(0)
                for h in range(8):
                    if h < 7:
                        weights(h + 1)
                    if h < 6:
                        maxima(h + 2)
                    dve.wait_ge(sem("at_out"), n * 8 + (h + 1))
                    V.tensor_copy(oT[:, h, ds(n * 128 + CTX, 128)], at_turn[0][:, 0:128]).then_inc(sem("at_kept"), 1)
                dve.sem_inc(sem("at_used"), 1)
            step.restart()
            dve.wait_ge(sem("at_kept"), 33)
            head_norm(40, 4, lambda n, b: one(oT, n, b), ONLY_LAT, lambda b: da_sg, None, rta, sqa, True)
            residual(O_DAOUT, ONLY_LAT, 64)
            norm(3, ONLY_LAT)
            peer(1, ONLY_LAT)


def kernel(**inputs):
    from concourse import bacc
    from concourse.bass_utils import run_bass_kernel_spmd

    f = {k: np.asarray(v) for k, v in inputs.items()}

    def tiles(w):
        return w.reshape(KC, 128, -1, 128).transpose(2, 1, 0, 3)

    def experts(u, v):
        u = u.reshape(128, 128, KC, 128).transpose(1, 3, 2, 0)
        v = v.reshape(128, 32, 4, 4, 2, 128).transpose(1, 3, 0, 4, 2, 5)
        return [u, v.reshape(128, 128, 8, 128)]

    def feature(v):
        return np.moveaxis(v.reshape(v.shape[:-1] + (KC, 128)), -1, 0)

    parts = [tiles(f["ada_w"][0]), tiles(f["ada_w"][1]), tiles(f["dn_w_in"][0][:, :4 * D]), tiles(f["dn_w_out"][0]),
             tiles(f["peer_wq"][0]), *experts(f["peer_u"][0], f["peer_v"][0]),
             tiles(f["da_w_qkv"][0]), tiles(f["da_w_out"][0]), tiles(f["peer_wq"][1]),
             *experts(f["peer_u"][1], f["peer_v"][1])]
    weights = np.concatenate(parts, 0)
    assert weights.shape[0] == 8 * O_END
    tokens = np.concatenate([f["ctx"][0], f["x"][0]], 0)
    rows = lambda v: np.broadcast_to(v.reshape(1, -1), (128, v.size))
    norms = np.stack([f["norm1_g"][0], f["norm2_g"][0], f["norm1_g"][1], f["norm2_g"][1]])
    params = np.concatenate([
        feature(np.stack([f["c"][0], f["c_ctx"]])).transpose(0, 2, 1).reshape(128, 16),
        f["ada_b"].reshape(96, 128).T,
        feature(norms).reshape(128, 32),
        f["dn_norm_g"][0][:, None], np.tile(f["da_q_norm_g"][0], 2)[:, None], np.tile(f["da_k_norm_g"][0], 2)[:, None],
        f["da_subln_g"][0][:, None],
        f["dn_conv"][0].reshape(5, 24, 128).transpose(2, 1, 0).reshape(128, 120),
        rows(f["dn_dt_bias"]), rows(f["dn_a_log"])], 1)
    where, const = const_table()
    arrays = {
        "weights": weights, "params": params, "const": const, "rope": rope_table(),
        "x": tokens.T.reshape(KC, 128, T).transpose(1, 0, 2),
        "w_ab": f["dn_w_in"][0][:, 4 * D:].reshape(KC, 128, 32).transpose(1, 0, 2),
        "lambdas": np.broadcast_to(f["da_lambda"][0].reshape(1, 256), (128, 256)),
        "keys": f["peer_keys"].reshape(2, 16, 128, 128).transpose(0, 3, 1, 2),
    }
    arrays = {k: np.ascontiguousarray(v) for k, v in arrays.items()}
    nc = bacc.Bacc("TRN2", target_bir_lowering=False, num_devices=1, dynamic_dma_scratch_size=1024)
    io = {k: nc.dram_tensor(f"in_{k}", v.shape, F32, kind="ExternalInput").ap() for k, v in arrays.items()}
    io["out"] = nc.dram_tensor("out_0", (128, KC, LAT), F32, kind="ExternalOutput").ap()
    backbone(nc, io, where)
    r = run_bass_kernel_spmd(nc, [{f"in_{k}": v for k, v in arrays.items()}], core_ids=[0])
    out = np.asarray(r.results[0]["out_0"])
    return np.ascontiguousarray(out.transpose(2, 1, 0).reshape(1, LAT, D))
```
